# Optimizing a Trainium2 kernel written in Bass

```python
import jax, jax.numpy as jnp
from jax import lax
import numpy as np

D_MODEL = 1024
BATCH = 1
SEQ = 512
DEPTH = 1
DEC_BATCH = 1
DEC_SEQ = 64
PAST_LEN = 128

CHUNK = 64
GLA_HEADS = 4
GLA_DK = D_MODEL // (2 * GLA_HEADS)
GLA_DV = D_MODEL // GLA_HEADS
GLA_RANK = 16
GLA_GATE_TAU = 16.0
DSA_HEADS = 8
DSA_KV_HEADS = 2
DSA_HEAD_DIM = 64
IDX_HEADS = 4
IDX_DIM = 64
IDX_SCALE = (IDX_HEADS * IDX_DIM) ** -0.5
TOPK_MAX = 256
QUERY_BLOCK = 128
FFN_DIM = 2816
CONV_W = 3
EPS = 1e-6
IN_SIZES = (GLA_HEADS * GLA_DK, GLA_HEADS * GLA_DK, GLA_HEADS * GLA_DV, GLA_RANK, GLA_HEADS * GLA_DV,
            DSA_HEADS * DSA_HEAD_DIM, DSA_KV_HEADS * DSA_HEAD_DIM, DSA_KV_HEADS * DSA_HEAD_DIM,
            IDX_HEADS * IDX_DIM, IDX_DIM, IDX_HEADS, 2 * D_MODEL)
D_IN = sum(IN_SIZES)

kernel_name = 'gla_dsa_convffn_stream_step'

def rmsnorm(x, g):
    xf = x.astype(jnp.float32)
    y = xf * lax.rsqrt(jnp.mean(xf * xf, axis=-1, keepdims=True) + EPS)
    return (y * g.astype(jnp.float32)).astype(x.dtype)

def gla_recurrence(q, k, v, log_a, s0):
    bsz, L, H, dk = q.shape
    dv = v.shape[-1]
    C = min(CHUNK, L)
    N = L // C

    def to_blocks(t):
        return t.astype(jnp.float32).reshape(bsz, N, C, H, t.shape[-1]).transpose(1, 0, 2, 3, 4)

    qc, kc, vc, gc = to_blocks(q), to_blocks(k), to_blocks(v), to_blocks(log_a)
    qc = qc * (dk ** -0.5)
    causal = jnp.tril(jnp.ones((C, C), dtype=bool))

    def step(S, inp):
        qi, ki, vi, gi = inp
        b = jnp.cumsum(gi, axis=1)
        b_last = b[:, -1]
        q_dec = qi * jnp.exp(b)
        k_inv = ki * jnp.exp(-b)
        scores = jnp.where(causal, jnp.einsum('bchd,bshd->bhcs', q_dec, k_inv), 0.0)
        o = jnp.einsum('bhcs,bshv->bchv', scores, vi) + jnp.einsum('bchd,bhdv->bchv', q_dec, S)
        k_rem = ki * jnp.exp(b_last[:, None] - b)
        S_new = jnp.exp(b_last)[..., None] * S + jnp.einsum('bchd,bchv->bhdv', k_rem, vi)
        return S_new, o

    s_fin, o = lax.scan(step, s0.astype(jnp.float32), (qc, kc, vc, gc))
    o = o.transpose(1, 0, 2, 3, 4).reshape(bsz, L, H, dv)
    return o, s_fin

def sparse_attend(q, q_idx, w_idx, q_pos, k_all, v_all, kidx_all, k_pos, topk):
    bsz, nq, hq, hd = q.shape
    f32 = jnp.float32
    dots = jnp.einsum('bqhd,bld->bqhl', q_idx.astype(f32), kidx_all.astype(f32))
    index_score = jnp.einsum('bqh,bqhl->bql', w_idx.astype(f32) * IDX_SCALE, jax.nn.relu(dots))
    admissible = (k_pos[None, :] // CHUNK) <= (q_pos[:, None] // CHUNK)
    index_score = jnp.where(admissible[None], index_score, -jnp.inf)
    _, sel = lax.top_k(index_score, topk)
    valid = (k_pos[sel] // CHUNK) <= (q_pos[None, :, None] // CHUNK)
    gather = jax.vmap(lambda t, i: t[i])
    k_sel = gather(k_all, sel).astype(f32)
    v_sel = gather(v_all, sel).astype(f32)
    qg = q.astype(f32).reshape(bsz, nq, DSA_KV_HEADS, hq // DSA_KV_HEADS, hd)
    logits = jnp.einsum('bqgrd,bqkgd->bqgrk', qg, k_sel) * (hd ** -0.5)
    logits = jnp.where(valid[:, :, None, None, :], logits, -jnp.inf)
    p = jax.nn.softmax(logits, axis=-1)
    o = jnp.einsum('bqgrk,bqkgd->bqgrd', p, v_sel)
    return o.reshape(bsz, nq, hq * hd)

def dsa_mixer(q, q_idx, w_idx, k_all, v_all, kidx_all, q_start):
    bsz, nq = q.shape[:2]
    n_keys = k_all.shape[1]
    topk = min(TOPK_MAX, n_keys // 4)
    k_pos = jnp.arange(n_keys)
    q_pos = q_start + jnp.arange(nq)
    qb = QUERY_BLOCK if nq % QUERY_BLOCK == 0 else nq
    nb = nq // qb

    def blockify(t):
        return t.reshape(bsz, nb, qb, *t.shape[2:]).swapaxes(0, 1)

    def one_block(args):
        qq, qi, ww, pp = args
        return sparse_attend(qq, qi, ww, pp, k_all, v_all, kidx_all, k_pos, topk)

    o = lax.map(one_block, (blockify(q), blockify(q_idx), blockify(w_idx), q_pos.reshape(nb, qb)))
    return o.swapaxes(0, 1).reshape(bsz, nq, -1)

def conv_ffn(xn, conv_prev, w_up, conv_w, conv_b, w_down):
    L = xn.shape[1]
    h = xn @ w_up
    hp = jnp.concatenate([conv_prev.astype(h.dtype), h], axis=1)
    hc = conv_b + sum(conv_w[j] * hp[:, j:j + L] for j in range(CONV_W))
    a, b = jnp.split(hc, 2, axis=-1)
    return (jax.nn.gelu(a) * b) @ w_down, hp[:, L:]

def run_layer(x, k_past, v_past, kidx_past, gla_s0, conv_prev,
              attn_pre_norm, w_in, w_gla_gate_up, b_gla_gate, gla_head_norm,
              w_branch_gla, w_branch_dsa, w_out, attn_post_norm,
              ffn_pre_norm, w_up, conv_w, conv_b, w_down, ffn_post_norm):
    bsz, L, _ = x.shape
    past = k_past.shape[1]
    xn = rmsnorm(x, attn_pre_norm)
    h = xn @ w_in
    splits = [int(s) for s in np.cumsum(IN_SIZES)[:-1]]
    (g_q, g_k, g_v, g_low, g_r, a_q, a_k, a_v, i_q, i_k, i_w, gate_logits) = jnp.split(h, splits, axis=-1)
    log_a = jax.nn.log_sigmoid((g_low @ w_gla_gate_up + b_gla_gate).astype(jnp.float32)) / GLA_GATE_TAU
    gla_o, gla_s = gla_recurrence(g_q.reshape(bsz, L, GLA_HEADS, GLA_DK),
                                  g_k.reshape(bsz, L, GLA_HEADS, GLA_DK),
                                  g_v.reshape(bsz, L, GLA_HEADS, GLA_DV),
                                  log_a.reshape(bsz, L, GLA_HEADS, GLA_DK), gla_s0)
    gla_o = rmsnorm(gla_o, gla_head_norm).reshape(bsz, L, GLA_HEADS * GLA_DV).astype(x.dtype) * jax.nn.silu(g_r)
    k_new = a_k.reshape(bsz, L, DSA_KV_HEADS, DSA_HEAD_DIM)
    v_new = a_v.reshape(bsz, L, DSA_KV_HEADS, DSA_HEAD_DIM)
    k_all = jnp.concatenate([k_past.astype(x.dtype), k_new], axis=1)
    v_all = jnp.concatenate([v_past.astype(x.dtype), v_new], axis=1)
    kidx_all = jnp.concatenate([kidx_past.astype(x.dtype), i_k], axis=1)
    dsa_o = dsa_mixer(a_q.reshape(bsz, L, DSA_HEADS, DSA_HEAD_DIM),
                      i_q.reshape(bsz, L, IDX_HEADS, IDX_DIM), i_w,
                      k_all, v_all, kidx_all, past).astype(x.dtype)
    gate_a, gate_b = jnp.split(jax.nn.sigmoid(gate_logits), 2, axis=-1)
    mixed = (gate_a * (gla_o @ w_branch_gla) + gate_b * (dsa_o @ w_branch_dsa)) @ w_out
    x = x + rmsnorm(mixed, attn_post_norm)
    f, conv_new = conv_ffn(rmsnorm(x, ffn_pre_norm), conv_prev, w_up, conv_w, conv_b, w_down)
    x = x + rmsnorm(f, ffn_post_norm)
    return x, k_new, v_new, i_k, gla_s, conv_new

def setup_inputs(seed: int = 0) -> dict:
    key = jax.random.key(seed)
    ks = jax.random.split(key, 24)
    nrm = jax.random.normal
    f32 = jnp.float32
    G, hd = DSA_KV_HEADS, DSA_HEAD_DIM

    def gain(k, n):
        return 1.0 + 0.02 * nrm(k, (DEPTH, n), f32)

    return {
        'x_prompt': nrm(ks[0], (BATCH, SEQ, D_MODEL), f32),
        'x_sample': nrm(ks[1], (DEC_BATCH, DEC_SEQ, D_MODEL), f32),
        'cache_k': nrm(ks[2], (DEPTH, DEC_BATCH, PAST_LEN, G, hd), f32),
        'cache_v': nrm(ks[3], (DEPTH, DEC_BATCH, PAST_LEN, G, hd), f32),
        'cache_k_idx': nrm(ks[4], (DEPTH, DEC_BATCH, PAST_LEN, IDX_DIM), f32),
        'state_gla': nrm(ks[5], (DEPTH, DEC_BATCH, GLA_HEADS, GLA_DK, GLA_DV), f32),
        'state_ffn_conv': nrm(ks[6], (DEPTH, DEC_BATCH, CONV_W - 1, 2 * FFN_DIM), f32),
        'attn_pre_norm': gain(ks[7], D_MODEL),
        'w_in': nrm(ks[8], (DEPTH, D_MODEL, D_IN), f32) * D_MODEL ** -0.5,
        'w_gla_gate_up': nrm(ks[9], (DEPTH, GLA_RANK, GLA_HEADS * GLA_DK), f32) * GLA_RANK ** -0.5,
        'b_gla_gate': 0.1 * nrm(ks[10], (DEPTH, GLA_HEADS * GLA_DK), f32),
        'gla_head_norm': gain(ks[11], GLA_DV),
        'w_branch_gla': nrm(ks[12], (DEPTH, GLA_HEADS * GLA_DV, D_MODEL), f32) * (GLA_HEADS * GLA_DV) ** -0.5,
        'w_branch_dsa': nrm(ks[13], (DEPTH, DSA_HEADS * hd, D_MODEL), f32) * (DSA_HEADS * hd) ** -0.5,
        'w_out': nrm(ks[14], (DEPTH, D_MODEL, D_MODEL), f32) * D_MODEL ** -0.5,
        'attn_post_norm': gain(ks[15], D_MODEL),
        'ffn_pre_norm': gain(ks[16], D_MODEL),
        'w_up': nrm(ks[17], (DEPTH, D_MODEL, 2 * FFN_DIM), f32) * D_MODEL ** -0.5,
        'conv_w': nrm(ks[18], (DEPTH, CONV_W, 2 * FFN_DIM), f32) * CONV_W ** -0.5,
        'conv_b': 0.02 * nrm(ks[19], (DEPTH, 2 * FFN_DIM), f32),
        'w_down': nrm(ks[20], (DEPTH, FFN_DIM, D_MODEL), f32) * FFN_DIM ** -0.5,
        'ffn_post_norm': gain(ks[21], D_MODEL),
    }

def reference(x_prompt, x_sample, cache_k, cache_v, cache_k_idx, state_gla, state_ffn_conv,
              attn_pre_norm, w_in, w_gla_gate_up, b_gla_gate, gla_head_norm,
              w_branch_gla, w_branch_dsa, w_out, attn_post_norm,
              ffn_pre_norm, w_up, conv_w, conv_b, w_down, ffn_post_norm):
    bsz = x_prompt.shape[0]
    dt = x_prompt.dtype
    y_prompt, y_sample = x_prompt, x_sample
    prompt_new, sample_new = [], []
    for l in range(DEPTH):
        lw = (attn_pre_norm[l], w_in[l], w_gla_gate_up[l], b_gla_gate[l], gla_head_norm[l],
              w_branch_gla[l], w_branch_dsa[l], w_out[l], attn_post_norm[l],
              ffn_pre_norm[l], w_up[l], conv_w[l], conv_b[l], w_down[l], ffn_post_norm[l])
        y_prompt, kp, vp, ip, sp, cp = run_layer(
            y_prompt,
            jnp.zeros((bsz, 0, DSA_KV_HEADS, DSA_HEAD_DIM), dt),
            jnp.zeros((bsz, 0, DSA_KV_HEADS, DSA_HEAD_DIM), dt),
            jnp.zeros((bsz, 0, IDX_DIM), dt),
            jnp.zeros((bsz, GLA_HEADS, GLA_DK, GLA_DV), jnp.float32),
            jnp.zeros((bsz, CONV_W - 1, 2 * FFN_DIM), dt),
            *lw)
        prompt_new.append((kp, vp, ip, sp, cp))
        y_sample, ksn, vsn, isn, ssn, csn = run_layer(
            y_sample, cache_k[l], cache_v[l], cache_k_idx[l], state_gla[l], state_ffn_conv[l], *lw)
        sample_new.append((ksn, vsn, isn, ssn, csn))
    k_p, v_p, kidx_p, gla_p, conv_p = (jnp.stack(t, axis=0) for t in zip(*prompt_new))
    k_s, v_s, kidx_s, gla_s, conv_s = (jnp.stack(t, axis=0) for t in zip(*sample_new))
    return (y_prompt, y_sample, k_p, v_p, kidx_p, gla_p, conv_p, k_s, v_s, kidx_s, gla_s, conv_s)


_drawn_inputs = setup_inputs


def setup_inputs(seed=0):
    import zlib

    import numpy as np

    out = dict(_drawn_inputs(seed))
    spreads = {}
    factors = {'gla_head_norm': 3.579,
     'attn_post_norm': 3.464,
     'ffn_pre_norm': 2.861,
     'conv_b': 3.493,
     'ffn_post_norm': 4.74}
    for name, (base, spread) in spreads.items():
        noise = np.random.default_rng([zlib.crc32(name.encode()), seed]).standard_normal(out[name].shape)
        drawn = base * np.exp(spread * noise) if base else spread * noise
        out[name] = __import__('jax').numpy.asarray(drawn.astype(out[name].dtype))
    for name, factor in factors.items():
        out[name] = (out[name] * factor).astype(out[name].dtype)
    return out
```

```python
from contextlib import ExitStack

import concourse.bass as bass
from concourse import mybir

F32 = mybir.dt.float32
F32R = mybir.dt.float32r
U32 = mybir.dt.uint32
ACT = mybir.ActivationFunctionType
ALU = mybir.AluOpType

P = 128
D = 1024
KD = D // P
SEQ = 512
DEC = 64
PAST = 128
T = DEC + SEQ
HALF = T // 2
CHUNK = 64
GH, DK, DV = 4, 128, 256
RANK = 16
TAU = 16.0
QH, KVH, HD = 8, 2, 64
IH, ID = 4, 64
IDX_SCALE = (IH * ID) ** -0.5
TOPK_P = min(256, SEQ // 4)
TOPK_S = min(256, (PAST + DEC) // 4)
FFN = 2816
KF = FFN // P
CW = 3
EPS = 1e-6
IN_SIZES = (GH * DK, GH * DK, GH * DV, RANK, GH * DV, QH * HD, KVH * HD, KVH * HD, IH * ID, ID, IH, 2 * D)
(O_GQ, O_GK, O_GV, O_LOW, O_GR, O_AQ, O_AK, O_AV, O_IQ, O_IK, O_IW, O_GATE) = [
    sum(IN_SIZES[:i]) for i in range(len(IN_SIZES))]
TILES = 5
NCH = T // CHUNK
TAKEN = -3.4e38
BARRED = -3.0e38
BIG = 1.0e30
CU = 2 + DEC + 2 + SEQ
UW = CU - 2


def tok(tt):
    return slice(0, P) if tt == 0 else slice(DEC + P * (tt - 1), DEC + P * tt)


def utok(tt):
    return slice(0, P) if tt == 0 else slice(DEC + 2 + P * (tt - 1), DEC + 2 + P * tt)


def rows(tt):
    return DEC if tt == 0 else P


def keys(tt):
    return slice(0, PAST + DEC) if tt == 0 else slice(PAST + DEC, PAST + DEC + P * tt)


def width(tt):
    return PAST + DEC if tt == 0 else P * tt


def key_blocks(tt):
    return [(0, P), (P, DEC)] if tt == 0 else [(P * b, P) for b in range(tt)]


PANELS = [("kv", 0), ("kv", 1), ("aq", 0), ("aq", 1), ("iq", 0)]
PANELS += [(k, i) for k, n in (("gq", 2), ("gk", 2), ("gv", 4), ("gr", 4), ("ga", 4), ("gb", 4)) for i in range(n)]
BRANCH0 = len(PANELS)
PANELS += [(k, i) for i in range(4) for k in ("wa", "wb")]
OUT0 = len(PANELS)
PANELS += [("out", i) for i in (0, 1, 2, 3, 0, 1)]
UP0 = len(PANELS)
PANELS += [("up", i) for i in range(KF)]
DOWN0 = len(PANELS)
DK_GROUPS = [(0, KF % 4)] + [(k, 4) for k in range(KF % 4, KF, 4)]
NG = len(DK_GROUPS)
PANELS += [("down", (n, k, c)) for n in range(2) for k, c in DK_GROUPS]
NP = len(PANELS)
FEAT = {"aq": (4, 2), "iq": (2, 2), "gq": (4, 2), "gk": (4, 2), "gr": (8, 2), "ga": (8, 2), "gb": (8, 2)}


class Job:
    def __init__(self, panel, n, k0, kn, tiles, banks, first, last):
        self.panel, self.n, self.k0, self.kn, self.tiles, self.banks = panel, n, k0, kn, tiles, banks
        self.first, self.last = first, last


OUT_JOBS = [Job(OUT0 + i, i // 2, 4 * (i % 2), 4, (0, 1, 2), (3 * (i // 2), 3 * (i // 2) + 1, 3 * (i // 2) + 2), i % 2 == 0, i % 2 == 1)
            for i in range(4)]
OUT_JOBS += [Job(OUT0 + 2 + i, 1, 4 * i, 4, (3, 4), (6, 7), i == 0, i == 1) for i in range(2)]
OUT_JOBS += [Job(OUT0 + 4 + i, 0, 4 * i, 4, (3, 4), (0, 1), i == 0, i == 1) for i in range(2)]
DOWN_JOBS = [Job(DOWN0 + n * NG + g, n, k, c, tuple(range(TILES)), tuple((5 * n + t) % 8 for t in range(TILES)), g == 0, g == NG - 1)
             for n in range(2) for g, (k, c) in enumerate(DK_GROUPS)]
JOBS = OUT_JOBS + DOWN_JOBS


def job_signal(job):
    i = JOBS.index(job)
    if job.last:
        return "wide_done", sum(len(j.tiles) for j in JOBS[:i + 1] if j.last)
    return "panel_used", 1 + sum(not j.last for j in JOBS[:i + 1])


def wide_order(job, t):
    return job_signal(job)[1] - len(job.tiles) + t + 1


class Slot:
    def __init__(self, kind, i, part, panel, opens, closes, unit, ends):
        self.kind, self.i, self.part, self.panel = kind, i, part, panel
        self.opens, self.closes, self.unit, self.ends = opens, closes, unit, ends


def plan_slots():
    slots, unit = [], 0

    def blocks(kind, which):
        nonlocal unit
        first = PANELS.index((kind, 0))
        for i in which:
            for j in range(2):
                slots.append(Slot(kind, i, j, first + i // 2, i % 2 == 0 and j == 0, i % 2 == 1 and j == 1, unit, j == 1))
            unit += 1

    for kind in ("aq", "iq", "gq", "gk"):
        blocks(kind, range(FEAT[kind][0]))
    for p in range(4):
        for tt in range(TILES):
            ends = tt % 2 == 1 or tt == TILES - 1
            slots.append(Slot("gv", p, tt, PANELS.index(("gv", p)), tt == 0, tt == TILES - 1, unit, ends))
            unit += ends
    for i in range(8):
        blocks("gr", [i])
        if i < GH:
            slots.append(Slot("z", i, 0, None, False, False, unit, True))
            unit += 1
    blocks("ga", range(8))
    blocks("gb", range(8))
    return slots, unit


SLOTS, UNITS1 = plan_slots()

IDX_TILES = [0, 2, 3, 4]
ATT_TILES = [1, 0, 2, 3, 4]
NATT = len(ATT_TILES) * QH
GLA_STEPS = [("a", 0), ("b", 0)] + [(s, t) for t in range(1, TILES) for s in "abc"]
AT_IDX, AT_ATT = 13, 17
AT_GLA = AT_ATT + NATT + 5
AT_NORM = AT_GLA + len(GLA_STEPS) + 1


def plan_aux():
    aux = {}

    def put(s, op):
        aux.setdefault(s, []).append(op)

    put(2, ("keyt", 0))
    for i in range(len(IDX_TILES)):
        put(AT_IDX + i, ("idx", i))
    for n in range(NATT + 3):
        put(AT_ATT + n, ("att", n))
    for i in range(len(GLA_STEPS)):
        put(AT_GLA + i, ("gla", i))
    put(0, ("coef", 0))
    put(AT_NORM, ("dsplit", 0))
    for h in range(GH):
        put(AT_NORM + 4 * h, ("square", h))
        put(AT_NORM + 4 * h + 1, ("norm", h))
        put(AT_NORM + 4 * h + 2, ("scale", h))
        put(AT_NORM + 4 * h + 4, ("gsplit", h))
    rounds = [(i, r) for i, tt in enumerate(IDX_TILES) for r in range((TOPK_S if tt == 0 else TOPK_P) // 8)]
    s = AT_IDX + 1
    for n in range(0, len(rounds), 2):
        i = rounds[n][0]
        s = max(s, AT_IDX + i + 1)
        put(s, ("topk", rounds[n:n + 2]))
        s += 1
    for n, s_ in enumerate(SLOTS):
        if s_.kind == "z":
            put(n, ("soft", s_.i))
            put(n + 1, ("decay", s_.i))
            put(n + 2, ("apply", s_.i))
    assert max(aux) < len(SLOTS), (max(aux), len(SLOTS))
    return aux


AUX = plan_aux()


def layer_kernel(nc, A, O):
    gate_dram = nc.dram_tensor("gate_scratch", (16, P, T), F32, kind="Internal").ap()
    silu_dram = nc.dram_tensor("silu_scratch", (8, P, T), F32, kind="Internal").ap()
    x1_dram = nc.dram_tensor("x1_scratch", (TILES, P, D), F32, kind="Internal").ap()

    with ExitStack() as ctx:
        base = (nc.sbuf_base + 63) // 64 * 64

        def at(name, shape, dtype, offset):
            size = 4
            for d in shape[1:]:
                size *= d
            assert base + offset + size <= nc.sbuf_usable_end, name
            return nc.alloc_sbuf_tensor_at(name, shape, dtype, offset=base + offset)

        def sem(name):
            return ctx.enter_context(nc.semaphore(name))

        ps = ctx.enter_context(nc.psum_tensor("ps", [P, 8, 512], F32))

        raw = at("raw", [P, 2, 2048], F32, 0)
        whi = at("whi", [P, 2, 2048], F32R, 16384)
        wlo = at("wlo", [P, 2, 2048], F32R, 32768)
        xhi = at("xhi", [P, KD, T], F32R, 49152)
        xlo = at("xlo", [P, KD, T], F32R, 67584)
        o = 86016
        ident = at("ident", [P, P], F32, o)
        ones = at("ones", [P, P], F32, o + 512)
        cmask = at("cmask", [P, GH, P], F32, o + 1024)
        restart = at("restart", [P, T], F32, o + 3072)
        cols = at("cols", [P, 288], F32, o + 5376)
        small = at("small", [P, 128], F32, o + 6528)
        ebl = at("ebl", [P, GH, NCH], F32, o + 7040)
        iws = at("iws", [P, TILES, IH], F32, o + 7200)
        convs = at("convs", [P, 4, 2 * KF], F32, o + 7296)
        o = 86016 + 8064
        v_tok = at("v_tok", [P, TILES, D], F32, o)
        x_tok = at("x_tok", [P, TILES, D], F32, o)
        ghi = at("ghi", [P, KD, T], F32R, o)
        qk = at("qk", [P, 2 * GH, T], F32, o + 20480)
        gq, gk, got = qk[:, 0:GH, :], qk[:, GH:2 * GH, :], qk
        gates_in = at("gates_in", [P, 4, T], F32, o + 20480)
        gpost = at("gpost", [P, D], F32, o + 20480 + 9216)
        gffn = at("gffn", [P, D], F32, o + 20480 + 9216 + 4096)
        o1 = o + 38912
        iz = at("iz", [P, 2, PAST + T], F32, o1)
        iqt = at("iqt", [P, 2, T], F32, o1 + 5632)
        krem = at("krem", [P, GH, T], F32, o1)
        kz = at("kz", [P, 2, PAST + T], F32, o1 + 10240)
        kvi = at("kvi", [P, TILES, 404], F32, o1 + 15872)
        cache = at("cache", [P, 3, P], F32, o1 + 23968)
        glow = at("glow", [P, T], F32, o1 + 25504)
        wgu = at("wgu", [P, GH * DK], F32, o1 + 27808)
        glo = at("glo", [P, KD, T], F32R, o1)
        dhi = at("dhi", [P, 4, T], F32R, o1 + 18432)
        x_re = at("x_re", [P, TILES, D], F32, o1)
        o2 = o1 + 29856
        aqt = at("aqt", [P, 4, T], F32, o2)
        state = at("state", [P, 2, GH, DV], F32, o2 + 9216)
        tmp = at("tmp", [P, 3, T], F32, o2 + 17408)
        stage = at("stage", [P, 2, T], F32, o2 + 24320)
        gpre = at("gpre", [P, D], F32, o2 + 24320)
        junk = at("junk", [P, D], F32, o2 + 17408)
        o3 = o2 + 28928
        score = [at(f"score{i}", [P, width(tt)], F32, o3 + off)
                 for i, (tt, off) in enumerate(zip(IDX_TILES, (0, 768, 1792, 3328)))]
        bias0 = at("bias0", [P, P], F32, o3 + 5376)
        lg = at("lg", [P, 2, 512], F32, o3 + 5888)
        pt = at("pt", [P, 2, 512], F32, o3 + 9984)
        otok = at("otok", [P, QH * HD], F32, o3 + 14080)
        relus = at("relus", [P, IH, 512], F32, o3 + 5888)
        coef_rows = at("coef_rows", [P, 3, P], F32, o3)
        scm = at("scm", [P, GH, P], F32, o3)
        krem_a = at("krem_a", [P, GH, P], F32, o3 + 2048)
        krem_b = at("krem_b", [P, GH, P], F32, o3 + 4096)
        qa = at("qa", [P, GH, P], F32, o3 + 6144)
        qb = at("qb", [P, GH, P], F32, o3 + 8192)
        dlo = at("dlo", [P, 4, T], F32R, o3)
        silu_in = at("silu_in", [P, 2, T], F32, o3 + 10240)
        y_tok = at("y_tok", [P, TILES, D], F32, o)
        xn_tok = at("xn_tok", [P, 2, D], F32, o3)
        uhi = at("uhi", [P, KF, UW], F32R, o)
        ulo = at("ulo", [P, KF, UW], F32R, o + 50880)
        o4 = o + 2 * 50880
        ha = at("ha", [P, 2, CU], F32, o4)
        hb = at("hb", [P, 2, CU], F32, o4 + 4640)
        ca = at("ca", [P, CU], F32, o4 + 9280)
        cb = at("cb", [P, UW], F32, o4 + 11616)
        conv_rows = at("conv_rows", [P, 2, P], F32, 49152 + 32768)
        y2_tok = at("y2_tok", [P, TILES, D], F32, 49152)
        x1_in = at("x1_in", [P, 2, D], F32, 49152 + 20480)
        gfin = at("gfin", [P, D], F32, 49152 + 28672)
        junk2 = at("junk2", [P, D], F32, o4)

        ssq, var, rstd = small[:, 0:5], small[:, 8:13], small[:, 16:21]
        negmax, rowsum, rinv = small[:, 24:26], small[:, 28:32], small[:, 32:34]
        m8, gnh = small[:, 40:48], small[:, 50:52]
        wsq, wsum = small[:, 56:66], small[:, 68:73]
        col_gate, col_hn = cols[:, 88:92], cols[:, 92:94]
        cw0, cw1, cw2, cbias = cols[:, 0:44], cols[:, 44:88], cols[:, 96:140], cols[:, 140:184]
        cstate = cols[:, 184:272]

        x_loaded = [sem(f"x_loaded{tt}") for tt in range(TILES)]
        gpre_loaded, coefs_loaded, cache_loaded = sem("gpre_loaded"), sem("coefs_loaded"), sem("cache_loaded")
        state_loaded = sem("state_loaded")
        raw_loaded = [sem("raw_loaded0"), sem("raw_loaded1")]
        hi_ready, lo_ready, panel_used = sem("hi_ready"), sem("lo_ready"), sem("panel_used")
        act_chain, dve_chain, pool_chain = sem("act_chain"), sem("dve_chain"), sem("pool_chain")
        consts_ready = sem("consts_ready")
        coefs_turned, coefs_ready = sem("coefs_turned"), sem("coefs_ready")
        ssq_primed = sem("ssq_primed")
        sumsq_ready, var_ready, root_ready, xn_ready = sem("sumsq_ready"), sem("var_ready"), sem("root_ready"), sem("xn_ready")
        x_turned, xhi_ready, xlo_ready = sem("x_turned"), sem("xhi_ready"), sem("xlo_ready")
        kv_done, kv_copied, keys_turned, keys_ready = sem("kv_done"), sem("kv_copied"), sem("keys_turned"), sem("keys_ready")
        unit_done, unit_free = sem("unit_done"), [sem("unit_free0"), sem("unit_free1")]
        tanh_ready, stage_saved = sem("tanh_ready"), [sem("stage_saved0"), sem("stage_saved1")]
        dots_done, relu_ready, scored = sem("dots_done"), sem("relu_ready"), sem("scored")
        logits_done, masked, probs_ready = sem("logits_done"), sem("masked"), sem("probs_ready")
        probs_turned, pt_ready, pv_done, o_scaled = sem("probs_turned"), sem("pt_ready"), sem("pv_done"), sem("o_scaled")
        o_turned, o_ready = sem("o_turned"), sem("o_ready")
        soft_ready, diff_ready = sem("soft_ready"), sem("diff_ready")
        decay_exp, decay_used = sem("decay_exp"), sem("decay_used")
        gla_a, gla_b, gla_c = sem("gla_scores_done"), sem("gla_chunk_a_done"), sem("gla_chunk_b_done")
        pads_zero, q_padded, krem_ready, sc_masked, state_ready, got_copied = (
            sem("pads_zero"), sem("q_padded"), sem("krem_ready"), sem("sc_masked"), sem("state_ready"), sem("got_copied"))
        sq_ready, norm_summed, head_var, head_root, head_out = (
            sem("sq_ready"), sem("norm_summed"), sem("head_var"), sem("head_root"), sem("head_out"))
        silu_loaded, ghi_ready, glo_ready, dhi_ready, dlo_ready = (
            sem("silu_loaded"), sem("ghi_ready"), sem("glo_ready"), sem("dhi_ready"), sem("dlo_ready"))
        gates_loaded = [sem("gates_loaded0"), sem("gates_loaded1")]
        merged, mhi_ready, mlo_ready = sem("merged"), sem("mhi_ready"), sem("mlo_ready")
        posts_loaded, x_reloaded = sem("posts_loaded"), sem("x_reloaded")
        wide_done, wide_squared, wide_free, ysum_ready, yroot_ready, x1_ready = (
            sem("wide_done"), sem("wide_squared"), sem("wide_free"), sem("ysum_ready"), sem("yroot_ready"), sem("x1_ready"))
        x1_sq, xvar_ready, xroot_ready, xn2_ready = sem("x1_sq"), sem("xvar_ready"), sem("xroot_ready"), sem("xn2_ready")
        x2_turned, x2hi_ready, x2lo_ready, x1_saved = sem("x2_turned"), sem("x2hi_ready"), sem("x2lo_ready"), sem("x1_saved")
        h_ready, rim_ready, ca_ready, gelu_ready, u_ready, uhi_ready, ulo_ready, tails_saved = (
            sem("h_ready"), sem("rim_ready"), sem("ca_ready"), sem("gelu_ready"), sem("u_ready"), sem("uhi_ready"), sem("ulo_ready"), sem("tails_saved"))
        tails_turned, tails_ready, gfin_loaded = sem("tails_turned"), sem("tails_ready"), sem("gfin_loaded")
        x1_loaded = [sem("x1_loaded0"), sem("x1_loaded1")]
        out_ready, stored, y_stored = sem("out_ready"), sem("stored"), sem("y_stored")

        w_in, w_up, w_down = A["w_in"][0], A["w_up"][0], A["w_down"][0]

        def cols_of(w, c0, n, k0=0, k=KD):
            return w[k0 * P:(k0 + k) * P, c0:c0 + n].rearrange("(k p) c -> p k c", p=P)

        def panel_loads(p):
            kind, i = PANELS[p]
            slot = raw[:, p % 2, :]

            def dst(k, n):
                return slot[:, 0:k * n].rearrange("p (k n) -> p k n", k=k)
            if kind == "kv":
                d = dst(4, 340)
                return [(d[:, :, 0:256], cols_of(w_in, O_AK, 256, 4 * i, 4)),
                        (d[:, :, 256:324], cols_of(w_in, O_IK, ID + IH, 4 * i, 4)),
                        (d[:, :, 324:340], cols_of(w_in, O_LOW, RANK, 4 * i, 4))]
            if kind == "aq":
                d = dst(KD, 256)
                return [(d[:, :, b * 128 + half * 64:b * 128 + half * 64 + 64],
                         cols_of(w_in, O_AQ + (2 * i + b + 4 * half) * HD, HD)) for b in range(2) for half in range(2)]
            simple = {"iq": O_IQ, "gq": O_GQ, "gk": O_GK, "gv": O_GV, "gr": O_GR, "ga": O_GATE, "gb": O_GATE + D}
            if kind in simple:
                return [(dst(KD, 256), cols_of(w_in, simple[kind] + 256 * i, 256))]
            if kind == "wa":
                return [(dst(KD, 256), cols_of(A["w_branch_gla"][0], 256 * i, 256))]
            if kind == "wb":
                return [(dst(4, 256), cols_of(A["w_branch_dsa"][0], 256 * i, 256, 0, 4))]
            if kind == "out":
                return [(dst(4, 512), cols_of(A["w_out"][0], 512 * (i // 2), 512, 4 * (i % 2), 4))]
            if kind == "up":
                d = dst(KD, 256)
                return [(d[:, :, 0:128], cols_of(w_up, i * P, P)), (d[:, :, 128:256], cols_of(w_up, FFN + i * P, P))]
            n, k, c = i
            return [(dst(c, 512), cols_of(w_down, 512 * n, 512, k, c))]

        def panel_size(p):
            kind, i = PANELS[p]
            return {"kv": 1360, "wb": 1024, "down": 512 * i[2] if kind == "down" else 0}.get(kind, 2048)

        def loaded(p):
            return 16 * sum(len(panel_loads(q)) for q in range(p % 2, p + 1, 2))

        def wait_panel_used(eng, p):
            kind, i = PANELS[p]
            if kind == "kv":
                eng.wait_ge(*((panel_used, 1) if i == 0 else (kv_done, TILES)))
            elif p < BRANCH0:
                eng.wait_ge(unit_done, 1 + max(s.unit for s in SLOTS if s.panel == p))
            elif p < OUT0:
                eng.wait_ge(unit_done, UNITS1 + 2 * (p - BRANCH0) + 2)
            elif UP0 <= p < DOWN0:
                eng.wait_ge(unit_done, UNITS2 + 2 * (p - UP0 + 1))
            else:
                name, value = job_signal([j for j in JOBS if j.panel == p][-1])
                eng.wait_ge({"wide_done": wide_done, "panel_used": panel_used}[name], value)

        def unit_waits(eng, unit):
            if unit >= 2:
                eng.wait_ge(unit_free[unit % 2], unit // 2)

        block = ctx.enter_context(nc.Block())

        def store_result(eng, tt):
            eng.wait_ge(out_ready, tt + 1)
            dst = O["y_s"][0] if tt == 0 else O["y_p"][0, P * (tt - 1):P * tt, :]
            eng.dma_start(dst, y2_tok[0:rows(tt), tt, :]).then_inc(y_stored, 16)

        @block.sync
        def _(sp):
            for tt in range(TILES):
                src = A["x_sample"][0] if tt == 0 else A["x_prompt"][0, P * (tt - 1):P * tt, :]
                sp.dma_start(x_tok[0:rows(tt), tt, :], src).then_inc(x_loaded[tt], 16)
            sp.dma_start(gpre[:, :], A["attn_pre_norm"][0].partition_broadcast(P)).then_inc(gpre_loaded, 16)
            for p in range(NP):
                if p >= 2:
                    sp.wait_ge(lo_ready, p - 1)
                for d, s in panel_loads(p):
                    sp.dma_start(d, s).then_inc(raw_loaded[p % 2], 16)
                if p == 1:
                    ck, cv = A["cache_k"][0, 0], A["cache_v"][0, 0]
                    sp.dma_start(cache[:, 0, :], ck.rearrange("s g d -> s (g d)")).then_inc(cache_loaded, 16)
                    sp.dma_start(cache[:, 1, :], cv.rearrange("s g d -> s (g d)")).then_inc(cache_loaded, 16)
                    for half in range(2):
                        sp.dma_start(cache[:, 2, half * 64:half * 64 + 64], A["cache_k_idx"][0, 0]).then_inc(cache_loaded, 16)
                    sp.wait_ge(pads_zero, 1)
                    sp.dma_start(wgu[0:RANK, :], A["w_gla_gate_up"][0]).then_inc(state_loaded, 16)
                    sp.dma_start(state[:, 0, :, :], A["state_gla"][0, 0].rearrange("h d v -> d h v")).then_inc(state_loaded, 16)
            sp.wait_ge(x1_saved, 16 * TILES)
            for tt in range(TILES):
                if tt < 2:
                    sp.wait_ge(h_ready, 2 * KF)
                else:
                    sp.wait_ge(out_ready, tt - 1)
                sp.dma_start(x1_in[0:rows(tt), tt % 2, :], x1_dram[tt, 0:rows(tt)]).then_inc(x1_loaded[tt % 2], 16)
                if tt >= 2:
                    store_result(sp, tt - 2)
            store_result(sp, TILES - 2)
            store_result(sp, TILES - 1)
            sp.wait_ge(y_stored, 16 * TILES)
            sp.wait_ge(stored, 16 * (8 + 2))

        @block.gpsimd
        def _(pool):
            chain = [0]

            def link(ins):
                chain[0] += 1
                ins.then_inc(pool_chain, 1)
                pool.wait_ge(pool_chain, chain[0])

            cwt = A["conv_w"][0].rearrange("j (b p) -> j b p", p=P)
            cst = A["state_ffn_conv"][0, 0].rearrange("j (b p) -> j b p", p=P)
            nb = 2 * KF
            link(nc.gpsimd.memset(ident[:, :], 0.0))
            nc.gpsimd.affine_select(out=ident[:, :], in_=ident[:, :], compare_op=ALU.not_equal, fill=1.0, base=0,
                                    pattern=[[-1, P]], channel_multiplier=1).then_inc(consts_ready, 1)
            for r, n, t, src in ((0, nb, 0, cwt[0]), (nb, nb, 0, cwt[1]),
                                 (2 * nb, 4, 0, A["b_gla_gate"][0].rearrange("(b p) -> b p", p=P)),
                                 (2 * nb + 4, 2, 0, A["gla_head_norm"].rearrange("l (b p) -> (l b) p", p=P)),
                                 (0, nb, 1, cwt[2]), (nb, nb, 1, A["conv_b"][0].rearrange("(b p) -> b p", p=P)),
                                 (0, nb, 2, cst[0]), (nb, nb, 2, cst[1])):
                pool.dma_start(coef_rows[r:r + n, t, :], src).then_inc(coefs_loaded, 16)
            nc.gpsimd.memset(ones[:, :], 1.0).then_inc(consts_ready, 1)
            link(nc.gpsimd.memset(cmask[:, :, :], 1.0))
            link(nc.gpsimd.affine_select(out=cmask[:, :, :], in_=cmask[:, :, :], compare_op=ALU.is_ge, fill=0.0, base=0,
                                         pattern=[[0, GH], [1, P]], channel_multiplier=-1))
            nc.gpsimd.memset(cmask[0:CHUNK, :, CHUNK:P], 0.0).then_inc(consts_ready, 1)
            link(nc.gpsimd.memset(restart[:, :], 1.0))
            nc.gpsimd.memset(restart[:, :].rearrange("p (n c) -> p n c", c=CHUNK)[:, :, 0:1], 0.0).then_inc(consts_ready, 1)
            nc.gpsimd.memset(wgu[:, :], 0.0).then_inc(pads_zero, 1)
            nc.gpsimd.memset(glow[:, :], 0.0).then_inc(pads_zero, 1)
            nc.gpsimd.memset(kz[:, :, :], 0.0).then_inc(pads_zero, 1)
            nc.gpsimd.memset(iz[:, :, :], 0.0).then_inc(pads_zero, 1)
            nc.gpsimd.memset(state[:, 1, :, :], 0.0).then_inc(pads_zero, 1)
            pool.wait_ge(coefs_turned, 1)
            link(nc.gpsimd.memset(bias0[:, :], 0.0))
            nc.gpsimd.memset(bias0[0:CHUNK, CHUNK:P], -BIG).then_inc(pads_zero, 1)

            pool.wait_ge(kv_copied, TILES)
            kp, vp, ip = (O[n][0, 0].rearrange("(t p) g d -> p t (g d)", p=P) if n != "kidx_p" else
                          O[n][0, 0].rearrange("(t p) d -> p t d", p=P) for n in ("k_p", "v_p", "kidx_p"))
            pool.dma_start(kp, kvi[:, 1:TILES, 0:128]).then_inc(stored, 16)
            pool.dma_start(vp, kvi[:, 1:TILES, 128:256]).then_inc(stored, 16)
            pool.dma_start(ip, kvi[:, 1:TILES, 256:320]).then_inc(stored, 16)
            pool.dma_start(O["k_s"][0, 0].rearrange("s g d -> s (g d)"), kvi[0:DEC, 0, 0:128]).then_inc(stored, 16)
            pool.dma_start(O["v_s"][0, 0].rearrange("s g d -> s (g d)"), kvi[0:DEC, 0, 128:256]).then_inc(stored, 16)
            pool.dma_start(O["kidx_s"][0, 0], kvi[0:DEC, 0, 256:320]).then_inc(stored, 16)

            staged = 0
            for s, slot in enumerate(SLOTS):
                if slot.kind in ("gr", "ga", "gb") and slot.ends:
                    pool.wait_ge(unit_free[slot.unit % 2], slot.unit // 2 + 1)
                    dst = silu_dram[slot.i] if slot.kind == "gr" else gate_dram[slot.i + (8 if slot.kind == "gb" else 0)]
                    pool.dma_start(dst, stage[:, staged % 2, :]).then_inc(stage_saved[staged % 2], 16)
                    staged += 1
                for op, n in AUX.get(s, []):
                    if op == "gla":
                        step, tt = GLA_STEPS[n]
                        if n == 0:
                            pool.wait_ge(o_ready, len(ATT_TILES))
                            for b in (scm, krem_a, krem_b, qa, qb):
                                nc.gpsimd.memset(b[:, :, :], 0.0).then_inc(pads_zero, 1)
                            pool.wait_ge(pads_zero, 11)
                            pool.wait_ge(decay_used, 3 * GH)
                        if step == "a":
                            if tt >= 1:
                                pool.wait_ge(gla_b, tt)
                            if tt >= 2:
                                pool.wait_ge(gla_c, tt - 1)
                            c0 = tok(tt).start
                            nc.gpsimd.tensor_copy(qa[:, :, 0:CHUNK], gq[:, :, c0:c0 + CHUNK]).then_inc(q_padded, 1)
                            nc.gpsimd.tensor_copy(qb[:, :, CHUNK:P], gq[:, :, c0 + CHUNK:c0 + P]).then_inc(q_padded, 1)
                    if op == "square":
                        pool.wait_ge(gla_c, TILES - 1)
                        if n == 0:
                            pool.wait_ge(stage_saved[0], 16 * 4)
                            pool.wait_ge(stage_saved[1], 16 * 4)
                        else:
                            pool.wait_ge(head_out, n)
                        pool.dma_start(silu_in[:, :, :], silu_dram[2 * n:2 * n + 2].rearrange("b p t -> p b t"))\
                            .then_inc(silu_loaded, 16)
            pool.wait_ge(state_ready, 2 * TILES - 1)
            pool.dma_start(O["gla_s"][0, 0].rearrange("h d v -> d h v"), state[:, 0, :, :]).then_inc(stored, 16)
            pool.dma_start(O["gla_p"][0, 0].rearrange("h d v -> d h v"), state[:, 1, :, :]).then_inc(stored, 16)
            pool.wait_ge(stage_saved[0], 16 * 12)
            pool.wait_ge(stage_saved[1], 16 * 12)
            pool.wait_ge(glo_ready, GH)
            for q in range(KD):
                m, g = 2 * (q // 2), q % 2
                if q >= 2:
                    for u in (UNITS1 + 2 * q - 4, UNITS1 + 2 * q - 3):
                        pool.wait_ge(unit_free[u % 2], u // 2 + 1)
                pool.dma_start(gates_in[:, 2 * g:2 * g + 2, :], gate_dram[8 * g + m:8 * g + m + 2].rearrange("b p t -> p b t"))\
                    .then_inc(gates_loaded[g], 16)
                if q == 0:
                    pool.dma_start(gpost[:, :], A["attn_post_norm"][0].partition_broadcast(P)).then_inc(posts_loaded, 16)
                    pool.dma_start(gffn[:, :], A["ffn_pre_norm"][0].partition_broadcast(P)).then_inc(posts_loaded, 16)
            wait_panel_used(pool, OUT0 - 1)
            pool.wait_ge(stored, 16 * 8)
            for tt in range(TILES):
                src = A["x_sample"][0] if tt == 0 else A["x_prompt"][0, P * (tt - 1):P * tt, :]
                pool.dma_start(x_re[0:rows(tt), tt, :], src).then_inc(x_reloaded, 16)
            for tt in range(TILES):
                pool.wait_ge(x1_ready, tt + 1)
                pool.dma_start(x1_dram[tt, 0:rows(tt)], x_re[0:rows(tt), tt, :]).then_inc(x1_saved, 16)
            pool.wait_ge(x2lo_ready, 2 * TILES)
            for i in range(2):
                for h in (ha, hb):
                    nc.gpsimd.memset(h[:, i, 2 + DEC:4 + DEC], 0.0).then_inc(pads_zero, 1)
            for j in range(KF):
                for g, h in enumerate((ha, hb)):
                    if j >= 2:
                        pool.wait_ge(ca_ready, 2 * (j - 2) + g + 1)
                    b = j + KF * g
                    rim = cstate.rearrange("p (i b) -> p i b", i=2)[:, :, b]
                    nc.gpsimd.tensor_copy(h[:, j % 2, 0:2], rim).then_inc(rim_ready, 1)
                for g, h in enumerate((ha, hb)):
                    b = j + KF * g
                    pool.wait_ge(h_ready, 2 * j + g + 1)
                    for i in range(2):
                        nc.gpsimd.tensor_copy(convs[:, 2 * i:2 * i + 2, b],
                                              h[:, j % 2, DEC + i * (CU - 2 - DEC):DEC + 2 + i * (CU - 2 - DEC)]).then_inc(tails_saved, 1)
            pool.dma_start(gfin[:, :], A["ffn_post_norm"][0].partition_broadcast(P)).then_inc(gfin_loaded, 16)
            pool.wait_ge(tails_ready, 1)
            pool.dma_start(O["conv_s"][0, 0].rearrange("j (b p) -> (j b) p", p=P), conv_rows[0:2 * nb, 0, :]).then_inc(stored, 16)
            pool.dma_start(O["conv_p"][0, 0].rearrange("j (b p) -> (j b) p", p=P), conv_rows[0:2 * nb, 1, :]).then_inc(stored, 16)

        @block.scalar
        def _(act):
            chain = [0]

            def link(ins):
                chain[0] += 1
                ins.then_inc(act_chain, 1)
                act.wait_ge(act_chain, chain[0])

            def split(p):
                if p >= NP:
                    return
                act.wait_ge(raw_loaded[p % 2], loaded(p))
                if p >= 2:
                    wait_panel_used(act, p - 2)
                n = panel_size(p)
                nc.scalar.activation(whi[:, p % 2, 0:n], raw[:, p % 2, 0:n], ACT.Copy).then_inc(hi_ready, 1)

            def feat(ap):
                return ap.rearrange("p (a b) -> p a b", a=2)

            act.wait_ge(ssq_primed, 1)

            def square(tt):
                act.wait_ge(x_loaded[tt], 16)
                nc.scalar.activation(junk[0:rows(tt), :], x_tok[0:rows(tt), tt, :], ACT.Square,
                                     accum_out=ssq[0:rows(tt), tt:tt + 1]).then_inc(sumsq_ready, 1)
                act.wait_ge(sumsq_ready, tt + 1)

            def root(tt):
                act.wait_ge(var_ready, tt + 1)
                nc.scalar.activation(rstd[:, tt:tt + 1], var[:, tt:tt + 1], ACT.Sqrt).then_inc(root_ready, 1)

            def turned(tt):
                for kh in range(2):
                    t = 2 * tt + kh
                    act.wait_ge(x_turned, t + 1)
                    n = rows(tt)
                    nc.scalar.activation(xhi[:, 4 * kh:4 * kh + 4, tok(tt).start:tok(tt).start + n],
                                         ps[:, 5 + t % 3, :].rearrange("p (k c) -> p k c", k=4)[:, :, 0:n], ACT.Copy).then_inc(xhi_ready, 1)

            square(0)
            root(0)
            for tt in range(1, TILES):
                square(tt)
                root(tt)
                if tt == 1:
                    split(0)
                turned(tt - 1)
            turned(TILES - 1)
            split(1)
            split(2)
            for tt in range(TILES):
                act.wait_ge(kv_done, tt + 1)
                nc.scalar.activation(kvi[:, tt, 0:320], ps[:, tt, 0:320], ACT.Copy)
                nc.scalar.activation(kvi[:, tt, 320:384], ps[:, tt, 256:320], ACT.Copy)
                nc.scalar.activation(kvi[:, tt, 384:404], ps[:, tt, 320:340], ACT.Copy).then_inc(kv_copied, 1)

            def copy_unit(slot):
                u, i = slot.unit, slot.i
                pair = 2 * (u % 2)
                src = ps[:, pair:pair + 2, 0:HALF]
                free = unit_free[u % 2]
                act.wait_ge(unit_done, u + 1)
                if slot.kind == "aq":
                    nc.scalar.activation(feat(aqt[:, i, :]), src, ACT.Copy).then_inc(free, 1)
                elif slot.kind == "iq":
                    nc.scalar.activation(feat(iqt[:, i, :]), src, ACT.Copy).then_inc(free, 1)
                elif slot.kind == "gq":
                    nc.scalar.activation(feat(gq[:, i, :]), src, ACT.Copy, scale=DK ** -0.5).then_inc(free, 1)
                elif slot.kind == "gk":
                    nc.scalar.activation(feat(gk[:, i, :]), src, ACT.Copy).then_inc(free, 1)
                elif slot.kind == "gv":
                    t0 = slot.part // 2 * 2
                    n = slot.part - t0 + 1
                    nc.scalar.activation(v_tok[:, t0:t0 + n, 256 * i:256 * i + 256], ps[:, pair:pair + n, 0:256],
                                         ACT.Copy).then_inc(free, 1)
                elif slot.kind == "z":
                    if i >= 1:
                        act.wait_ge(decay_used, 3 * i)
                    nc.scalar.activation(feat(tmp[:, 0, :]), src, ACT.Identity, bias=col_gate[:, i:i + 1]).then_inc(free, 1)
                else:
                    n = {"gr": 0, "ga": 8, "gb": 16}[slot.kind] + i
                    if n >= 2:
                        act.wait_ge(stage_saved[n % 2], 16 * (n // 2))
                    nc.scalar.activation(feat(stage[:, n % 2, :]), src, ACT.Tanh, scale=0.5)\
                        .then_inc(tanh_ready if slot.kind == "gr" else free, 1)

            def aux(op, n):
                if op == "coef":
                    act.wait_ge(coefs_turned, 1)
                    nc.scalar.activation(cols[:, 0:94], ps[:, 7, 0:94], ACT.Copy)
                    nc.scalar.activation(cols[:, 96:272], ps[:, 7, 96:272], ACT.Copy).then_inc(coefs_ready, 1)
                elif op == "keyt":
                    act.wait_ge(keys_turned, 1)
                    act.wait_ge(pads_zero, 4)
                    for g in range(2):
                        r = slice(64 * g, 64 * g + 64)
                        nc.scalar.activation(kz[r, g, PAST + DEC:], ps[r, 5, :], ACT.Copy)
                        nc.scalar.activation(iz[r, g, PAST + DEC:], ps[r, 6, :], ACT.Copy)
                        nc.scalar.activation(kz[r, g, 0:PAST + DEC], ps[r, 7, 0:PAST + DEC], ACT.Copy)
                        nc.scalar.activation(iz[r, g, 0:PAST + DEC], ps[r, 7, PAST + DEC:2 * (PAST + DEC)], ACT.Copy)
                    nc.scalar.activation(glow[0:RANK, DEC:T], ps[0:RANK, 4, :], ACT.Copy)
                    nc.scalar.activation(glow[0:RANK, 0:DEC], ps[0:RANK, 7, 384:448], ACT.Copy).then_inc(keys_ready, 1)
                elif op == "idx":
                    w = width(IDX_TILES[n])
                    act.wait_ge(dots_done, n + 1)
                    if n >= 1:
                        act.wait_ge(scored, n)
                    for h in range(IH):
                        nc.scalar.activation(relus[:, h, 0:w], ps[:, 4 + h, 0:w], ACT.Relu).then_inc(relu_ready, 1)
                elif op == "att":
                    if n < NATT:
                        w = width(ATT_TILES[n // QH])
                        act.wait_ge(masked, n + 1)
                        nc.scalar.activation(lg[:, n % 2, 0:w], lg[:, n % 2, 0:w], ACT.Exp, bias=negmax[:, n % 2:n % 2 + 1],
                                             scale=-1.0, accum_out=rowsum[:, n % 4:n % 4 + 1]).then_inc(probs_ready, 1)
                    m = n - 1
                    if 0 <= m < NATT:
                        tt = ATT_TILES[m // QH]
                        act.wait_ge(probs_turned, m + 1)
                        if m >= 2:
                            act.wait_ge(pv_done, m - 1)
                        if tt == 0:
                            nc.scalar.activation(pt[:, m % 2, 0:P], ps[:, 6, 0:P], ACT.Copy)
                            ins = nc.scalar.activation(pt[0:DEC, m % 2, P:2 * P], ps[0:DEC, 6, P:2 * P], ACT.Copy)
                        else:
                            ins = nc.scalar.activation(pt[:, m % 2, 0:P * tt], ps[:, 6, 0:P * tt], ACT.Copy)
                        ins.then_inc(pt_ready, 1)
                    m = n - 3
                    if m >= 0 and m % QH == QH - 1:
                        t = m // QH
                        tt = ATT_TILES[t]
                        act.wait_ge(o_turned, t + 1)
                        k = rows(tt)
                        nc.scalar.activation(aqt[:, :, tok(tt).start:tok(tt).start + k],
                                             ps[:, 4 + (n + 1) % 2, :].rearrange("p (b c) -> p b c", b=4)[:, :, 0:k], ACT.Copy).then_inc(o_ready, 1)
                elif op == "soft":
                    z, a, b = tmp[:, 0, :], tmp[:, 1, :], tmp[:, 2, :]
                    act.wait_ge(unit_free[Z_UNIT[n] % 2], Z_UNIT[n] // 2 + 1)
                    link(nc.scalar.activation(a, z, ACT.Abs))
                    link(nc.scalar.activation(a, a, ACT.Exp, scale=-1.0))
                    nc.scalar.activation(a, a, ACT.Ln, bias=1.0).then_inc(soft_ready, 1)
                elif op == "decay":
                    z, a, b = tmp[:, 0, :], tmp[:, 1, :], tmp[:, 2, :]
                    act.wait_ge(diff_ready, n + 1)
                    nc.scalar.activation(b, b, ACT.Exp, scale=1.0 / TAU).then_inc(decay_exp, 1)
                    nc.scalar.activation(z, a, ACT.Exp, scale=1.0 / TAU).then_inc(decay_exp, 1)
                    link(nc.scalar.activation(ebl[:, n, :], a.rearrange("p (n c) -> p n c", c=CHUNK)[:, :, CHUNK - 1],
                                              ACT.Exp, scale=1.0 / TAU))
                    act.wait_ge(decay_exp, 3 * n + 2)
                    nc.scalar.activation(a, a, ACT.Exp, scale=-1.0 / TAU).then_inc(decay_exp, 1)
                elif op == "gla":
                    step, tt = GLA_STEPS[n]
                    if step == "a":
                        act.wait_ge(gla_a, tt + 1)
                        act.wait_ge(pads_zero, 11)
                        nc.scalar.activation(krem_a[0:CHUNK, :, :], ps[0:CHUNK, 4, :].rearrange("p (h d) -> p h d", h=GH), ACT.Copy)\
                            .then_inc(krem_ready, 1)
                        nc.scalar.activation(krem_b[CHUNK:P, :, :], ps[CHUNK:P, 4, :].rearrange("p (h d) -> p h d", h=GH), ACT.Copy)\
                            .then_inc(krem_ready, 1)
                    elif step == "c" or tt == 0:
                        if tt == 0:
                            act.wait_ge(gla_b, 1)
                        else:
                            act.wait_ge(gla_c, tt)
                        k = rows(tt)
                        nc.scalar.activation(got[:, :, tok(tt).start:tok(tt).start + k],
                                             ps[:, 6:8, :].rearrange("p a (b c) -> p (a b) c", b=4)[:, :, 0:k], ACT.Copy)\
                            .then_inc(got_copied, 1)
                elif op == "square":
                    if n >= 1:
                        act.wait_ge(norm_summed, n)
                    act.wait_ge(got_copied, TILES)
                    nc.scalar.activation(tmp[:, 0:2, :], got[:, 2 * n:2 * n + 2, :], ACT.Square).then_inc(sq_ready, 1)
                elif op == "norm":
                    act.wait_ge(head_var, n + 1)
                    nc.scalar.activation(tmp[:, 2, :], tmp[:, 2, :], ACT.Sqrt).then_inc(head_root, 1)
                elif op == "gsplit":
                    act.wait_ge(head_out, n + 1)
                    nc.scalar.activation(ghi[:, 2 * n:2 * n + 2, :], got[:, 2 * n:2 * n + 2, :], ACT.Copy).then_inc(ghi_ready, 1)
                elif op == "dsplit":
                    act.wait_ge(stored, 16 * 6)
                    nc.scalar.activation(dhi[:, :, :], aqt[:, :, :], ACT.Copy).then_inc(dhi_ready, 1)

            for s, slot in enumerate(SLOTS):
                if slot.opens and slot.panel > 1:
                    split(slot.panel + 1)
                if slot.ends:
                    copy_unit(slot)
                for op, n in AUX.get(s, []):
                    aux(op, n)
            for q in range(KD // 2):
                split(BRANCH0 + 2 * q + 1)
                split(BRANCH0 + 2 * q + 2)
                for m in (2 * q, 2 * q + 1):
                    act.wait_ge(merged, m + 1)
                    nc.scalar.activation(xhi[:, m, :], tmp[:, m % 2, :], ACT.Copy, scale=0.5).then_inc(mhi_ready, 1)

            def row_squares(job, t, jk):
                i = wide_order(job, t)
                tt = job.tiles[t]
                act.wait_ge(wide_done, i)
                nc.scalar.activation(jk[:, 0:512], ps[:, job.banks[t], :], ACT.Square,
                                     accum_out=wsq[:, 2 * tt + job.n:2 * tt + job.n + 1]).then_inc(wide_squared, 1)
                act.wait_ge(wide_squared, i)

            def row_root(tt, base):
                act.wait_ge(ysum_ready, base + tt + 1)
                nc.scalar.activation(wsum[:, tt:tt + 1], wsum[:, tt:tt + 1], ACT.Sqrt).then_inc(yroot_ready, 1)

            def second_squares(tt):
                act.wait_ge(x1_ready, tt + 1)
                k = rows(tt)
                nc.scalar.activation(junk[0:k, :], x_re[0:k, tt, :], ACT.Square, accum_out=ssq[0:k, tt:tt + 1]).then_inc(x1_sq, 1)
                act.wait_ge(x1_sq, tt + 1)
                act.wait_ge(xvar_ready, tt + 1)
                nc.scalar.activation(rstd[0:k, tt:tt + 1], var[0:k, tt:tt + 1], ACT.Sqrt).then_inc(xroot_ready, 1)

            def second_hi(tt):
                k = rows(tt)
                for kh in range(2):
                    act.wait_ge(x2_turned, 2 * tt + kh + 1)
                    nc.scalar.activation(xhi[:, 4 * kh:4 * kh + 4, tok(tt).start:tok(tt).start + k],
                                         ps[:, TURN_BANKS[tt][kh], :].rearrange("p (k c) -> p k c", k=4)[:, :, 0:k], ACT.Copy)\
                        .then_inc(x2hi_ready, 1)

            for what, *n in OUT_PLAN:
                if what == "split":
                    split(n[0])
                elif what == "evac":
                    row_squares(OUT_JOBS[n[0]], n[1], junk)
                elif what == "residual":
                    row_root(n[0], 0)
                elif what == "norm":
                    second_squares(n[0])
                else:
                    second_hi(n[0])
            for j in range(KF):
                if j:
                    split(UP0 + j + 1)
                for g, h in enumerate((ha, hb)):
                    u = 2 * j + g
                    pair = 4 * (j % 2) + 2 * g
                    act.wait_ge(unit_done, UNITS2 + u + 1)
                    if j == 0 and g == 0:
                        act.wait_ge(x1_saved, 16 * TILES)
                    if j >= 2:
                        act.wait_ge(ca_ready, 2 * (j - 2) + g + 1)
                        act.wait_ge(tails_saved, 4 * (j - 2) + 2 * g + 2)
                    nc.scalar.activation(h[:, j % 2, 2:2 + DEC], ps[:, pair, 0:DEC], ACT.Copy)
                    nc.scalar.activation(h[:, j % 2, 4 + DEC:4 + HALF], ps[:, pair, DEC:HALF], ACT.Copy)
                    nc.scalar.activation(h[:, j % 2, 4 + HALF:CU], ps[:, pair + 1, 0:HALF], ACT.Copy).then_inc(h_ready, 1)
                act.wait_ge(ca_ready, 2 * j + 1)
                nc.scalar.activation(ca[:, 0:UW], ca[:, 0:UW], ACT.Gelu_apprx_tanh).then_inc(gelu_ready, 1)
                act.wait_ge(u_ready, j + 1)
                nc.scalar.activation(uhi[:, j, :], ca[:, 0:UW], ACT.Copy).then_inc(uhi_ready, 1)
            for q, job in enumerate(DOWN_JOBS):
                split(job.panel + 1)
                if q == 1:
                    act.wait_ge(tails_turned, 1)
                    nc.scalar.activation(conv_rows[0:4 * KF, :, :], ps[0:4 * KF, 7, 0:256].rearrange("p (a b) -> p a b", a=2), ACT.Copy)\
                        .then_inc(tails_ready, 1)
                if job.last:
                    for t in range(TILES):
                        row_squares(job, t, junk2)
                        if job.n == 1:
                            row_root(t, TILES)

        @block.vector
        def _(dve):
            chain = [0]

            def link(ins):
                chain[0] += 1
                ins.then_inc(dve_chain, 1)
                dve.wait_ge(dve_chain, chain[0])

            def split(p):
                if p >= NP:
                    return
                dve.wait_ge(hi_ready, p + 1)
                n = panel_size(p)
                nc.vector.tensor_tensor(wlo[:, p % 2, 0:n], raw[:, p % 2, 0:n], whi[:, p % 2, 0:n].bitcast(F32),
                                        ALU.subtract).then_inc(lo_ready, 1)

            def feat(ap):
                return ap.rearrange("p (a b) -> p a b", a=2)

            def head(tt):
                k = rows(tt)
                dve.wait_ge(sumsq_ready, tt + 1)
                c = slice(tt, tt + 1)
                nc.vector.tensor_scalar(var[:, c], ssq[:, c], 1.0 / D, EPS, ALU.mult, ALU.add).then_inc(var_ready, 1)
                dve.wait_ge(root_ready, tt + 1)
                link(nc.vector.reciprocal(rstd[:, c], rstd[:, c]))
                if tt == 0:
                    dve.wait_ge(gpre_loaded, 16)
                nc.vector.scalar_tensor_tensor(out=x_tok[0:k, tt, :], in0=x_tok[0:k, tt, :], scalar=rstd[0:k, c],
                                               in1=gpre[0:k, :], op0=ALU.mult, op1=ALU.mult).then_inc(xn_ready, 1)

            def rest(tt):
                for kh in range(2):
                    t = 2 * tt + kh
                    k = rows(tt)
                    dve.wait_ge(xhi_ready, t + 1)
                    c = slice(tok(tt).start, tok(tt).start + k)
                    nc.vector.tensor_tensor(xlo[:, 4 * kh:4 * kh + 4, c], ps[:, 5 + t % 3, :].rearrange("p (k c) -> p k c", k=4)[:, :, 0:k],
                                            xhi[:, 4 * kh:4 * kh + 4, c].bitcast(F32), ALU.subtract).then_inc(xlo_ready, 1)

            nc.vector.memset(ssq, 1.0).then_inc(ssq_primed, 1)
            head(0)
            for tt in range(1, TILES):
                head(tt)
                if tt == 1:
                    split(0)
                rest(tt - 1)
            rest(TILES - 1)
            split(1)
            split(2)
            dve.wait_ge(kv_copied, TILES)
            link(nc.vector.tensor_scalar(iws[:, :, :], kvi[:, :, 384:388], IDX_SCALE, None, ALU.mult))

            def gla_update(stream, chunk):
                for h in range(GH):
                    ins = nc.vector.scalar_tensor_tensor(
                        out=state[:, stream, h, :], in0=state[:, stream, h, :], scalar=ebl[:, h, chunk:chunk + 1],
                        in1=ps[:, 4 + h // 2, 256 * (h % 2):256 * (h % 2) + 256], op0=ALU.mult, op1=ALU.add)
                ins.then_inc(state_ready, 1)

            def aux(op, n):
                if op == "coef":
                    dve.wait_ge(coefs_ready, 1)
                    link(nc.vector.tensor_scalar(gnh, col_hn, 0.5, None, ALU.mult))
                elif op == "idx":
                    tt = IDX_TILES[n]
                    w = width(tt)
                    sc = score[n]
                    dve.wait_ge(relu_ready, 4 * n + 1)
                    link(nc.vector.tensor_scalar(sc[:, :], relus[:, 0, 0:w], iws[:, tt, 0:1], None, ALU.mult))
                    for h in range(1, IH):
                        dve.wait_ge(relu_ready, 4 * n + h + 1)
                        ins = nc.vector.scalar_tensor_tensor(out=sc[:, :], in0=relus[:, h, 0:w], scalar=iws[:, tt, h:h + 1],
                                                             in1=sc[:, :], op0=ALU.mult, op1=ALU.add)
                        if h < IH - 1 or tt:
                            link(ins)
                    if tt:
                        ins = nc.vector.memset(sc[0:CHUNK, w - CHUNK:w], BARRED)
                    ins.then_inc(scored, 1)
                    dve.wait_ge(scored, n + 1)
                elif op == "topk":
                    for i, r in n:
                        sc = score[i]
                        link(nc.vector.max(m8, sc[:, :]))
                        link(nc.vector.match_replace(sc[:, :], m8, sc[:, :], TAKEN))
                        if r == (TOPK_S if IDX_TILES[i] == 0 else TOPK_P) // 8 - 1:
                            link(nc.vector.tensor_scalar(sc[:, :], sc[:, :], TAKEN, -BIG, ALU.not_equal, ALU.mult))
                elif op == "att":
                    if n < NATT:
                        tt = ATT_TILES[n // QH]
                        w = width(tt)
                        bias = bias0 if tt == 1 else score[IDX_TILES.index(tt)]
                        dve.wait_ge(logits_done, n + 1)
                        if n == 0:
                            dve.wait_ge(pads_zero, 6)
                        if n >= 2:
                            dve.wait_ge(probs_turned, n - 1)
                        nc.vector.tensor_tensor_reduce(out=lg[:, n % 2, 0:w], in0=ps[:, 4 + n % 2, 0:w], in1=bias[:, 0:w],
                                                       scale=-HD ** -0.5, scalar=3.0e38, op0=ALU.add, op1=ALU.min,
                                                       accum_out=negmax[:, n % 2:n % 2 + 1]).then_inc(masked, 1)
                    m = n - 2
                    if 0 <= m < NATT:
                        h = m % QH
                        dve.wait_ge(probs_ready, m + 1)
                        link(nc.vector.reciprocal(rinv[:, m % 2:m % 2 + 1], rowsum[:, m % 4:m % 4 + 1]))
                        dve.wait_ge(pv_done, m + 1)
                        if m >= QH and h == 0:
                            dve.wait_ge(o_turned, m // QH)
                        g = h // (QH // KVH)
                        nc.vector.tensor_scalar(otok[:, HD * h:HD * h + HD], ps[:, 7, HD * g:HD * g + HD],
                                                rinv[:, m % 2:m % 2 + 1], None, ALU.mult).then_inc(o_scaled, 1)
                elif op == "soft":
                    z, a, b = tmp[:, 0, :], tmp[:, 1, :], tmp[:, 2, :]
                    dve.wait_ge(soft_ready, n + 1)
                    link(nc.vector.scalar_tensor_tensor(out=z, in0=z, scalar=0.0, in1=a, op0=ALU.min, op1=ALU.subtract))
                    link(nc.vector.tensor_tensor_scan(a, restart[:, :], z, 0.0, ALU.mult, ALU.add))
                    ac = a.rearrange("p (n c) -> p n c", c=CHUNK)
                    nc.vector.tensor_tensor(b.rearrange("p (n c) -> p n c", c=CHUNK),
                                            ac[:, :, CHUNK - 1:CHUNK].to_broadcast([P, NCH, CHUNK]), ac, ALU.subtract).then_inc(diff_ready, 1)
                elif op == "apply":
                    z, a, b = tmp[:, 0, :], tmp[:, 1, :], tmp[:, 2, :]
                    dve.wait_ge(decay_exp, 3 * n + 1)
                    nc.vector.tensor_tensor(krem[:, n, :], gk[:, n, :], b, ALU.mult).then_inc(decay_used, 1)
                    dve.wait_ge(decay_exp, 3 * n + 2)
                    nc.vector.tensor_tensor(gq[:, n, :], gq[:, n, :], z, ALU.mult).then_inc(decay_used, 1)
                    dve.wait_ge(decay_exp, 3 * n + 3)
                    nc.vector.tensor_tensor(gk[:, n, :], gk[:, n, :], a, ALU.mult).then_inc(decay_used, 1)
                elif op == "gla":
                    step, tt = GLA_STEPS[n]
                    if step == "a":
                        dve.wait_ge(gla_a, tt + 1)
                        dve.wait_ge(pads_zero, 11)
                        nc.vector.copy_predicated(scm[:, :, :], cmask[:, :, :].bitcast(U32),
                                                  ps[:, 5, :].rearrange("p (h c) -> p h c", h=GH)).then_inc(sc_masked, 1)
                    elif step == "b":
                        dve.wait_ge(gla_b, tt + 1)
                        gla_update(0 if tt == 0 else 1, 0 if tt == 0 else 2 * tt - 1)
                    else:
                        dve.wait_ge(gla_c, tt)
                        dve.wait_ge(state_ready, 2 * tt)
                        gla_update(1, 2 * tt)
                elif op == "norm":
                    rs = tmp[:, 2, :]
                    dve.wait_ge(norm_summed, n + 1)
                    nc.vector.tensor_scalar(feat(rs), ps[:, 4:6, 0:HALF], 1.0 / DV, EPS, ALU.mult, ALU.add).then_inc(head_var, 1)
                elif op == "scale":
                    rs = tmp[:, 2, :]
                    dve.wait_ge(head_root, n + 1)
                    link(nc.vector.reciprocal(rs, rs))
                    dve.wait_ge(silu_loaded, 16 * (n + 1))
                    for d in range(2):
                        y = got[:, 2 * n + d, :]
                        link(nc.vector.tensor_tensor(y, y, rs, ALU.mult))
                        ins = nc.vector.scalar_tensor_tensor(out=y, in0=y, scalar=gnh[:, d:d + 1], in1=silu_in[:, d, :],
                                                             op0=ALU.mult, op1=ALU.mult)
                    ins.then_inc(head_out, 1)
                elif op == "gsplit":
                    dve.wait_ge(ghi_ready, n + 1)
                    nc.vector.tensor_tensor(glo[:, 2 * n:2 * n + 2, :], got[:, 2 * n:2 * n + 2, :],
                                            ghi[:, 2 * n:2 * n + 2, :].bitcast(F32), ALU.subtract).then_inc(glo_ready, 1)
                elif op == "dsplit":
                    dve.wait_ge(dhi_ready, 1)
                    nc.vector.tensor_tensor(dlo[:, :, :], aqt[:, :, :], dhi[:, :, :].bitcast(F32), ALU.subtract).then_inc(dlo_ready, 1)

            for s, slot in enumerate(SLOTS):
                if slot.opens and slot.panel > 1:
                    split(slot.panel + 1)
                if slot.kind == "gr" and slot.ends:
                    pair = 2 * (slot.unit % 2)
                    dve.wait_ge(tanh_ready, slot.i + 1)
                    st = feat(stage[:, slot.i % 2, :])
                    nc.vector.scalar_tensor_tensor(out=st, in0=st, scalar=1.0, in1=ps[:, pair:pair + 2, 0:HALF],
                                                   op0=ALU.add, op1=ALU.mult).then_inc(unit_free[slot.unit % 2], 1)
                for op, n in AUX.get(s, []):
                    aux(op, n)
            for q in range(KD // 2):
                for g in range(2):
                    split(BRANCH0 + 2 * q + g + 1)
                    for m in (2 * q, 2 * q + 1):
                        u = UNITS1 + 4 * q + 2 * g + m % 2
                        dve.wait_ge(unit_done, u + 1)
                        if m % 2 == 0:
                            dve.wait_ge(gates_loaded[g], 16 * (q + 1))
                        if m >= 2 and g == 0:
                            dve.wait_ge(mhi_ready, m - 1)
                            dve.wait_ge(mlo_ready, m - 1)
                        if m % 2 == 1 and g == 1:
                            dve.wait_ge(merged, m)
                        dst = tmp[:, m % 2 if g == 0 else 2, :]
                        nc.vector.scalar_tensor_tensor(out=feat(dst), in0=feat(gates_in[:, 2 * g + m % 2, :]), scalar=1.0,
                                                       in1=ps[:, 2 * (u % 2):2 * (u % 2) + 2, 0:HALF], op0=ALU.add, op1=ALU.mult)\
                            .then_inc(unit_free[u % 2], 1)
                        if g == 1:
                            dve.wait_ge(unit_free[u % 2], u // 2 + 1)
                            f = tmp[:, m % 2, :]
                            nc.vector.tensor_tensor(f, f, tmp[:, 2, :], ALU.add).then_inc(merged, 1)
                for m in (2 * q, 2 * q + 1):
                    dve.wait_ge(mhi_ready, m + 1)
                    nc.vector.scalar_tensor_tensor(out=xlo[:, m, :], in0=tmp[:, m % 2, :], scalar=0.5, in1=xhi[:, m, :].bitcast(F32),
                                                   op0=ALU.mult, op1=ALU.subtract).then_inc(mlo_ready, 1)

            def wide_copy(job, t, y, gain):
                tt = job.tiles[t]
                c = slice(512 * job.n, 512 * job.n + 512)
                dve.wait_ge(wide_squared, wide_order(job, t))
                nc.vector.tensor_tensor(y[:, tt, c], ps[:, job.banks[t], :], gain[:, c], ALU.mult).then_inc(wide_free, 1)

            def row_scale(tt, base, copied):
                dve.wait_ge(wide_free, copied)
                link(nc.vector.tensor_tensor(wsum[:, tt:tt + 1], wsq[:, 2 * tt:2 * tt + 1], wsq[:, 2 * tt + 1:2 * tt + 2], ALU.add))
                nc.vector.tensor_scalar(wsum[:, tt:tt + 1], wsum[:, tt:tt + 1], 1.0 / D, EPS, ALU.mult, ALU.add).then_inc(ysum_ready, 1)
                dve.wait_ge(yroot_ready, base + tt + 1)
                link(nc.vector.reciprocal(wsum[:, tt:tt + 1], wsum[:, tt:tt + 1]))

            def residual(tt, copied):
                k = rows(tt)
                row_scale(tt, 0, copied)
                nc.vector.scalar_tensor_tensor(out=x_re[0:k, tt, :], in0=y_tok[0:k, tt, :], scalar=wsum[0:k, tt:tt + 1],
                                               in1=x_re[0:k, tt, :], op0=ALU.mult, op1=ALU.add).then_inc(x1_ready, 1)

            def second_norm(tt):
                k = rows(tt)
                dve.wait_ge(x1_sq, tt + 1)
                nc.vector.tensor_scalar(var[0:k, tt:tt + 1], ssq[0:k, tt:tt + 1], 1.0 / D, EPS, ALU.mult, ALU.add).then_inc(xvar_ready, 1)
                dve.wait_ge(xroot_ready, tt + 1)
                link(nc.vector.reciprocal(rstd[0:k, tt:tt + 1], rstd[0:k, tt:tt + 1]))
                if tt >= 2:
                    dve.wait_ge(x2_turned, 2 * tt - 2)
                nc.vector.scalar_tensor_tensor(out=xn_tok[0:k, tt % 2, :], in0=x_re[0:k, tt, :], scalar=rstd[0:k, tt:tt + 1],
                                               in1=gffn[0:k, :], op0=ALU.mult, op1=ALU.mult).then_inc(xn2_ready, 1)

            def second_lo(tt):
                k = rows(tt)
                for kh in range(2):
                    c = slice(tok(tt).start, tok(tt).start + k)
                    dve.wait_ge(x2hi_ready, 2 * tt + kh + 1)
                    nc.vector.tensor_tensor(xlo[:, 4 * kh:4 * kh + 4, c],
                                            ps[:, TURN_BANKS[tt][kh], :].rearrange("p (k c) -> p k c", k=4)[:, :, 0:k],
                                            xhi[:, 4 * kh:4 * kh + 4, c].bitcast(F32), ALU.subtract).then_inc(x2lo_ready, 1)

            dve.wait_ge(posts_loaded, 32)
            closed = 0
            for what, *n in OUT_PLAN:
                if what == "split":
                    split(n[0])
                elif what == "evac":
                    wide_copy(OUT_JOBS[n[0]], n[1], y_tok, gpost)
                    closed += 1
                elif what == "residual":
                    if n[0] == 0:
                        dve.wait_ge(x_reloaded, 16 * TILES)
                    residual(n[0], closed)
                elif what == "norm":
                    second_norm(n[0])
                else:
                    second_lo(n[0])
            for j in range(KF):
                if j:
                    split(UP0 + j + 1)
                for g, (h, c) in enumerate(((ha, ca), (hb, cb))):
                    b = j + KF * g
                    dve.wait_ge(h_ready, 2 * j + g + 1)
                    dve.wait_ge(rim_ready, 2 * j + g + 1)
                    if j == 0:
                        dve.wait_ge(pads_zero, 15)
                    if g == 0 and j >= 1:
                        dve.wait_ge(uhi_ready, j)
                        dve.wait_ge(ulo_ready, j)
                    cc = c[:, 0:UW]
                    hr = h[:, j % 2, :]
                    link(nc.vector.tensor_scalar(cc, hr[:, 2:CU], cw2[:, b:b + 1], cbias[:, b:b + 1], ALU.mult, ALU.add))
                    link(nc.vector.scalar_tensor_tensor(out=cc, in0=hr[:, 1:CU - 1], scalar=cw1[:, b:b + 1], in1=cc, op0=ALU.mult, op1=ALU.add))
                    nc.vector.scalar_tensor_tensor(out=cc, in0=hr[:, 0:CU - 2], scalar=cw0[:, b:b + 1], in1=cc, op0=ALU.mult, op1=ALU.add)\
                        .then_inc(ca_ready, 1)
                dve.wait_ge(gelu_ready, j + 1)
                dve.wait_ge(ca_ready, 2 * j + 2)
                nc.vector.tensor_tensor(ca[:, 0:UW], ca[:, 0:UW], cb[:, :], ALU.mult).then_inc(u_ready, 1)
                dve.wait_ge(uhi_ready, j + 1)
                nc.vector.tensor_tensor(ulo[:, j, :], ca[:, 0:UW], uhi[:, j, :].bitcast(F32), ALU.subtract).then_inc(ulo_ready, 1)
            for job in DOWN_JOBS:
                split(job.panel + 1)
                if job.last:
                    for t in range(TILES):
                        if job.n == 0 and t == 0:
                            dve.wait_ge(gfin_loaded, 16)
                        wide_copy(job, t, y2_tok, gfin)
                        if job.n == 1:
                            k = rows(t)
                            row_scale(t, TILES, wide_order(job, t))
                            dve.wait_ge(x1_loaded[t % 2], 16 * (t // 2 + 1))
                            nc.vector.scalar_tensor_tensor(out=y2_tok[0:k, t, :], in0=y2_tok[0:k, t, :], scalar=wsum[0:k, t:t + 1],
                                                           in1=x1_in[0:k, t % 2, :], op0=ALU.mult, op1=ALU.add).then_inc(out_ready, 1)

        @block.tensor
        def _(pe):
            def open_panel(p):
                pe.wait_ge(lo_ready, p + 1)

            def half_of(w, p, k, n):
                return w[:, p % 2, 0:k * n].rearrange("p (k n) -> p k n", k=k)

            def stationary_weights(out, p, kn, n, c0, xh, xl, t):
                wh, wl = half_of(whi, p, kn, n), half_of(wlo, p, kn, n)
                for k in range(kn):
                    pe.matmul(out, wh[:, k, c0:c0 + P], xh[:, k, t], start=(k == 0), stop=False)
                    pe.matmul(out, wh[:, k, c0:c0 + P], xl[:, k, t], start=False, stop=False)
                    ins = pe.matmul(out, wl[:, k, c0:c0 + P], xh[:, k, t], start=False, stop=(k == kn - 1))
                return ins

            def moving_weights(out, p, k0, kn, n, xh, xl, t, first, last):
                wh, wl = half_of(whi, p, kn, n), half_of(wlo, p, kn, n)
                for k in range(kn):
                    pe.matmul(out, xh[:, k0 + k, t], wh[:, k, :], start=(first and k == 0), stop=False)
                    pe.matmul(out, xl[:, k0 + k, t], wh[:, k, :], start=False, stop=False)
                    ins = pe.matmul(out, xh[:, k0 + k, t], wl[:, k, :], start=False, stop=(last and k == kn - 1))
                return ins

            def turn(tt):
                k = rows(tt)
                pe.wait_ge(xn_ready, tt + 1)
                for kh in range(2):
                    t = 2 * tt + kh
                    if t >= 3:
                        pe.wait_ge(xlo_ready, t - 2)
                    for j in range(4):
                        f = 4 * kh + j
                        ins = pe.transpose(ps[:, 5 + t % 3, P * j:P * j + k], x_tok[0:k, tt, P * f:P * f + P], ident[0:k, 0:k])
                    ins.then_inc(x_turned, 1)

            def keys_values(p, tt):
                if tt == 0:
                    open_panel(p)
                pe.wait_ge(xlo_ready, 2 * max(tt, 1) + 2)
                return moving_weights(ps[:, tt, 0:340], p, 4 * p, 4, 340, xhi, xlo, tok(tt), p == 0, p == 1)

            pe.wait_ge(consts_ready, 1)
            turn(0)
            turn(1)
            for tt in range(TILES):
                if tt + 2 < TILES:
                    turn(tt + 2)
                ins = keys_values(0, tt)
            ins.then_inc(panel_used, 1)
            for tt in range(TILES):
                keys_values(1, tt).then_inc(kv_done, 1)

            def main(slot):
                u = slot.unit
                pair = 2 * (u % 2)
                if slot.opens:
                    open_panel(slot.panel)
                starts = slot.part % 2 == 0
                if starts:
                    unit_waits(pe, u)
                    if u < 2:
                        pe.wait_ge(kv_copied, 2 * u + 2)
                if slot.kind == "z":
                    for j in range(2):
                        ins = pe.matmul(ps[:, pair + j, 0:HALF], wgu[:, P * slot.i:P * slot.i + P],
                                        glow[:, HALF * j:HALF * j + HALF], start=True, stop=True)
                elif slot.kind == "gv":
                    ins = moving_weights(ps[:, pair + slot.part % 2, 0:256], slot.panel, 0, KD, 256, xhi, xlo,
                                         tok(slot.part), True, True)
                else:
                    ins = stationary_weights(ps[:, pair + slot.part, 0:HALF], slot.panel, KD, 256, P * (slot.i % 2),
                                             xhi, xlo, slice(HALF * slot.part, HALF * slot.part + HALF))
                if slot.ends:
                    ins.then_inc(unit_done, 1)

            def state_products(kr, tt):
                for h in range(GH):
                    ins = pe.matmul(ps[:, 4 + h // 2, 256 * (h % 2):256 * (h % 2) + 256], kr[:, h, :],
                                    v_tok[:, tt, 256 * h:256 * h + 256], start=True, stop=True)
                return ins

            def outputs_of_state(stream, q, last):
                for h in range(GH):
                    for d in range(2):
                        r = 2 * (h % 2) + d
                        ins = pe.matmul(ps[:, 6 + h // 2, P * r:P * r + P], state[:, stream, h, P * d:P * d + P], q[:, h, :],
                                        start=False, stop=last, skip_group_check=True)
                return ins

            def aux(op, n):
                if op == "coef":
                    pe.wait_ge(coefs_loaded, 16 * 8)
                    pe.transpose(ps[:, 7, 0:94], coef_rows[0:94, 0, :], ident[0:94, 0:94])
                    pe.transpose(ps[:, 7, 96:184], coef_rows[0:88, 1, :], ident[0:88, 0:88])
                    pe.transpose(ps[:, 7, 184:272], coef_rows[0:88, 2, :], ident[0:88, 0:88]).then_inc(coefs_turned, 1)
                elif op == "keyt":
                    pe.wait_ge(coefs_ready, 1)
                    pe.wait_ge(consts_ready, 4)
                    pe.wait_ge(kv_copied, TILES)
                    pe.wait_ge(cache_loaded, 16 * 4)
                    for tt in range(1, TILES):
                        c = slice(P * (tt - 1), P * tt)
                        pe.transpose(ps[:, 5, c], kvi[:, tt, 0:128], ident[:, :])
                        pe.transpose(ps[:, 6, c], kvi[:, tt, 256:384], ident[:, :])
                        pe.transpose(ps[0:RANK, 4, c], kvi[:, tt, 388:404], ident[:, :])
                    i64 = ident[0:DEC, 0:DEC]
                    pe.transpose(ps[:, 7, 0:128], cache[:, 0, :], ident[:, :])
                    pe.transpose(ps[:, 7, 128:192], kvi[0:DEC, 0, 0:128], i64)
                    pe.transpose(ps[:, 7, 192:320], cache[:, 2, :], ident[:, :])
                    pe.transpose(ps[:, 7, 320:384], kvi[0:DEC, 0, 256:384], i64)
                    pe.transpose(ps[0:RANK, 7, 384:448], kvi[0:DEC, 0, 388:404], i64).then_inc(keys_turned, 1)
                elif op == "idx":
                    tt = IDX_TILES[n]
                    w = width(tt)
                    if n == 0:
                        pe.wait_ge(keys_ready, 1)
                        pe.wait_ge(unit_free[0], 3)
                        pe.wait_ge(unit_free[1], 3)
                    else:
                        pe.wait_ge(relu_ready, 4 * n)
                    for h in range(IH):
                        ins = pe.matmul(ps[:, 4 + h, 0:w], iqt[:, h // 2, tok(tt)], iz[:, h % 2, keys(tt)], start=True, stop=True)
                    ins.then_inc(dots_done, 1)
                elif op == "att":
                    if n < NATT:
                        tt = ATT_TILES[n // QH]
                        w = width(tt)
                        h = n % QH
                        if n == 0:
                            pe.wait_ge(relu_ready, 4 * len(IDX_TILES))
                            pe.wait_ge(scored, len(IDX_TILES))
                        if n >= 2:
                            pe.wait_ge(masked, n - 1)
                        if n >= 11 and (n - 4) % QH == QH - 1:
                            pe.wait_ge(o_ready, (n - 4) // QH + 1)
                        pe.matmul(ps[:, 4 + n % 2, 0:w], aqt[:, h % 4, tok(tt)], kz[:, h // 4, keys(tt)],
                                  start=True, stop=True).then_inc(logits_done, 1)
                    m = n - 1
                    if 0 <= m < NATT:
                        pe.wait_ge(probs_ready, m + 1)
                        if m >= 1:
                            pe.wait_ge(pt_ready, m)
                        for i, (c, k) in enumerate(key_blocks(ATT_TILES[m // QH])):
                            ins = pe.transpose(ps[0:k, 6, P * i:P * i + P], lg[:, m % 2, c:c + k], ident[:, :])
                        ins.then_inc(probs_turned, 1)
                    m = n - 2
                    if 0 <= m < NATT:
                        tt = ATT_TILES[m // QH]
                        pe.wait_ge(pt_ready, m + 1)
                        if m >= 1:
                            pe.wait_ge(o_scaled, m)
                        blocks = key_blocks(tt)
                        for i, (c, k) in enumerate(blocks):
                            if tt == 0:
                                val = cache[:, 1, :] if i == 0 else kvi[0:DEC, 0, 128:256]
                            else:
                                val = kvi[:, i + 1, 128:256]
                            ins = pe.matmul(ps[:, 7, 0:128], pt[0:k, m % 2, P * i:P * i + P], val,
                                            start=(i == 0), stop=(i == len(blocks) - 1))
                        ins.then_inc(pv_done, 1)
                    m = n - 3
                    if m >= 0 and m % QH == QH - 1:
                        pe.wait_ge(o_scaled, m + 1)
                        for b in range(4):
                            ins = pe.transpose(ps[:, 4 + (n + 1) % 2, P * b:P * b + P], otok[:, P * b:P * b + P], ident[:, :])
                        ins.then_inc(o_turned, 1)
                elif op == "gla":
                    step, tt = GLA_STEPS[n]
                    stream = 0 if tt == 0 else 1
                    if step == "a":
                        if n == 0:
                            pe.wait_ge(decay_used, 3 * GH)
                            pe.wait_ge(o_ready, len(ATT_TILES))
                        else:
                            pe.wait_ge(state_ready, 1 if tt == 1 else 2 * tt - 1)
                        for h in range(GH):
                            pe.transpose(ps[:, 4, P * h:P * h + P], krem[:, h, tok(tt)], ident[:, :])
                        for h in range(GH):
                            ins = pe.matmul(ps[:, 5, P * h:P * h + P], gk[:, h, tok(tt)], gq[:, h, tok(tt)], start=True, stop=True)
                        ins.then_inc(gla_a, 1)
                    elif step == "b":
                        if tt == 0:
                            pe.wait_ge(state_loaded, 32)
                        if tt >= 1:
                            pe.wait_ge(got_copied, tt)
                            pe.wait_ge(state_ready, 1 if tt == 1 else 2 * tt - 1)
                        pe.wait_ge(sc_masked, tt + 1)
                        pe.wait_ge(q_padded, 2 * tt + 2)
                        for h in range(GH):
                            for d in range(2):
                                r = 2 * (h % 2) + d
                                pe.matmul(ps[:, 6 + h // 2, P * r:P * r + P], v_tok[:, tt, 256 * h + P * d:256 * h + P * d + P],
                                          scm[:, h, :], start=(r == 0), stop=False, skip_group_check=True)
                        outputs_of_state(stream, qa, tt == 0)
                        pe.wait_ge(krem_ready, 2 * tt + 2)
                        state_products(krem_a, tt).then_inc(gla_b, 1)
                    else:
                        pe.wait_ge(state_ready, 2 * tt)
                        outputs_of_state(stream, qb, True)
                        state_products(krem_b, tt).then_inc(gla_c, 1)
                elif op == "norm":
                    pe.wait_ge(sq_ready, n + 1)
                    if n == 0:
                        pe.wait_ge(state_ready, 2 * TILES - 1)
                    else:
                        pe.wait_ge(head_var, n)
                    for j in range(2):
                        for d in range(2):
                            ins = pe.matmul(ps[:, 4 + j, 0:HALF], ones[:, :], tmp[:, d, HALF * j:HALF * j + HALF],
                                            start=(d == 0), stop=(d == 1))
                    ins.then_inc(norm_summed, 1)

            for s, slot in enumerate(SLOTS):
                main(slot)
                for op, n in AUX.get(s, []):
                    aux(op, n)
            pe.wait_ge(glo_ready, GH)
            pe.wait_ge(dlo_ready, 1)
            for q in range(KD // 2):
                for g in range(2):
                    p = BRANCH0 + 2 * q + g
                    open_panel(p)
                    for m in range(2):
                        u = UNITS1 + 4 * q + 2 * g + m
                        unit_waits(pe, u)
                        for j in range(2):
                            xh, xl, kn = (ghi, glo, KD) if g == 0 else (dhi, dlo, 4)
                            ins = stationary_weights(ps[:, 2 * (u % 2) + j, 0:HALF], p, kn, 256, P * m, xh, xl,
                                                     slice(HALF * j, HALF * j + HALF))
                        ins.then_inc(unit_done, 1)

            def wide(job, xh, xl, tk):
                open_panel(job.panel)
                for t, tt in enumerate(job.tiles):
                    if job.first:
                        wait_bank(job, t)
                    ins = moving_weights(ps[:, job.banks[t], :], job.panel, job.k0, job.kn, 512, xh, xl, tk(tt), job.first, job.last)
                    if job.last:
                        ins.then_inc(wide_done, 1)
                if not job.last:
                    ins.then_inc(panel_used, 1)

            def wait_bank(job, t):
                before = [wide_order(j, i) for j in JOBS[:JOBS.index(job)] if j.last
                          for i, b in enumerate(j.banks) if b == job.banks[t]]
                if before:
                    pe.wait_ge(wide_free, before[-1])

            def turn_again(tt):
                k = rows(tt)
                pe.wait_ge(xn2_ready, tt + 1)
                pe.wait_ge(wide_free, 10 if tt == 3 else 8 if tt == 4 else 6)
                if tt >= 2:
                    pe.wait_ge(x2lo_ready, {2: 2, 3: 6, 4: 4}[tt])
                for kh in range(2):
                    for j in range(4):
                        f = 4 * kh + j
                        ins = pe.transpose(ps[:, TURN_BANKS[tt][kh], P * j:P * j + k], xn_tok[0:k, tt % 2, P * f:P * f + P],
                                           ident[0:k, 0:k])
                    ins.then_inc(x2_turned, 1)

            pe.wait_ge(unit_free[0], UNITS2 // 2)
            pe.wait_ge(unit_free[1], UNITS2 // 2)
            for q, job in enumerate(OUT_JOBS):
                pe.wait_ge(mlo_ready, 8 if job.k0 else 4)
                wide(job, xhi, xlo, tok)
                if q >= 5:
                    turn_again(q - 5)

            def up(j, g, t):
                return stationary_weights(ps[:, 4 * (j % 2) + 2 * g + t, 0:HALF], UP0 + j, KD, 256, P * g, xhi, xlo,
                                          slice(HALF * t, HALF * t + HALF))

            pe.wait_ge(x2lo_ready, 6)
            pe.wait_ge(wide_free, 10)
            for j in range(2):
                open_panel(UP0 + j)
                for g in range(2):
                    up(j, g, 0)
                turn_again(3 + j)
            pe.wait_ge(x2lo_ready, 2 * TILES)
            for j in range(2):
                for g in range(2):
                    up(j, g, 1).then_inc(unit_done, 1)
            for j in range(2, KF):
                open_panel(UP0 + j)
                for g in range(2):
                    pe.wait_ge(h_ready, 2 * (j - 2) + g + 1)
                    up(j, g, 0)
                    up(j, g, 1).then_inc(unit_done, 1)
            pe.wait_ge(h_ready, 2 * KF)
            for q, job in enumerate(DOWN_JOBS):
                pe.wait_ge(ulo_ready, job.k0 + job.kn)
                wide(job, uhi, ulo, utok)
                if q == 0:
                    pe.wait_ge(tails_saved, 4 * KF)
                    for i in range(2):
                        ins = pe.transpose(ps[0:4 * KF, 7, P * i:P * i + P], convs[:, 2 * i:2 * i + 2, :].rearrange("p a b -> p (a b)"),
                                           ident[:, :])
                    ins.then_inc(tails_turned, 1)
                if q == NG - 1:
                    pe.wait_ge(tails_ready, 1)


UNITS2 = UNITS1 + 2 * KD
TURN_BANKS = [(2, 3), (4, 5), (2, 3), (1, 3), (5, 7)]
OUT_PLAN = [("split", OUT0 + 1), ("split", OUT0 + 2), ("evac", 1, 0), ("evac", 1, 1), ("evac", 1, 2), ("split", OUT0 + 3),
            ("evac", 3, 0), ("residual", 0), ("evac", 3, 1), ("residual", 1), ("norm", 0), ("evac", 3, 2), ("residual", 2),
            ("norm", 1), ("split", OUT0 + 4), ("turned", 0), ("norm", 2), ("evac", 5, 0), ("evac", 5, 1), ("split", OUT0 + 5),
            ("turned", 1), ("turned", 2), ("split", UP0), ("evac", 7, 0), ("residual", 3), ("norm", 3), ("evac", 7, 1), ("residual", 4),
            ("split", UP0 + 1), ("norm", 4), ("turned", 3), ("turned", 4)]
Z_UNIT = [s.unit for s in SLOTS if s.kind == "z"]

_INS = ['x_prompt', 'x_sample', 'cache_k', 'cache_v', 'cache_k_idx', 'state_gla', 'state_ffn_conv', 'attn_pre_norm', 'w_in',
        'w_gla_gate_up', 'b_gla_gate', 'gla_head_norm', 'w_branch_gla', 'w_branch_dsa', 'w_out', 'attn_post_norm',
        'ffn_pre_norm', 'w_up', 'conv_w', 'conv_b', 'w_down', 'ffn_post_norm']
_OUTS = [("y_p", (1, SEQ, D)), ("y_s", (1, DEC, D)),
         ("k_p", (1, 1, SEQ, KVH, HD)), ("v_p", (1, 1, SEQ, KVH, HD)), ("kidx_p", (1, 1, SEQ, ID)),
         ("gla_p", (1, 1, GH, DK, DV)), ("conv_p", (1, 1, CW - 1, 2 * FFN)),
         ("k_s", (1, 1, DEC, KVH, HD)), ("v_s", (1, 1, DEC, KVH, HD)), ("kidx_s", (1, 1, DEC, ID)),
         ("gla_s", (1, 1, GH, DK, DV)), ("conv_s", (1, 1, CW - 1, 2 * FFN))]


def kernel(**inputs):
    import numpy as np
    import concourse.bacc as bacc
    from concourse.bass_utils import run_bass_kernel_spmd

    nc = bacc.Bacc("TRN2", target_bir_lowering=False, num_devices=1)
    arrays, A, O = {}, {}, {}
    for name in _INS:
        a = np.ascontiguousarray(inputs[name])
        arrays[f"in_{name}"] = a
        A[name] = nc.dram_tensor(f"in_{name}", a.shape, F32, kind="ExternalInput").ap()
    for name, shape in _OUTS:
        O[name] = nc.dram_tensor(f"out_{name}", shape, F32, kind="ExternalOutput").ap()
    layer_kernel(nc, A, O)
    r = run_bass_kernel_spmd(nc, [arrays], core_ids=[0])
    return tuple(r.results[0][f"out_{name}"] for name, _ in _OUTS)
```

```python
from contextlib import ExitStack

import concourse.bass as bass
from concourse import mybir

F32 = mybir.dt.float32
F32R = mybir.dt.float32r
U32 = mybir.dt.uint32
ACT = mybir.ActivationFunctionType
ALU = mybir.AluOpType

P = 128
D = 1024
KD = D // P
SEQ = 512
DEC = 64
PAST = 128
T = DEC + SEQ
HALF = T // 2
CHUNK = 64
GH, DK, DV = 4, 128, 256
RANK = 16
TAU = 16.0
QH, KVH, HD = 8, 2, 64
IH, ID = 4, 64
IDX_SCALE = (IH * ID) ** -0.5
TOPK_P = min(256, SEQ // 4)
TOPK_S = min(256, (PAST + DEC) // 4)
FFN = 2816
KF = FFN // P
CW = 3
EPS = 1e-6
IN_SIZES = (GH * DK, GH * DK, GH * DV, RANK, GH * DV, QH * HD, KVH * HD, KVH * HD, IH * ID, ID, IH, 2 * D)
(O_GQ, O_GK, O_GV, O_LOW, O_GR, O_AQ, O_AK, O_AV, O_IQ, O_IK, O_IW, O_GATE) = [
    sum(IN_SIZES[:i]) for i in range(len(IN_SIZES))]
TILES = 5
NCH = T // CHUNK
TAKEN = -3.4e38
BARRED = -3.0e38
BIG = 1.0e30
CU = 2 + DEC + 2 + SEQ
UW = CU - 2


def tok(tt):
    return slice(0, P) if tt == 0 else slice(DEC + P * (tt - 1), DEC + P * tt)


def prompt(tt, first):
    return slice(first + P * (tt - 1), first + P * tt)


def rows(tt):
    return DEC if tt == 0 else P


def keys(tt):
    return slice(0, PAST + DEC) if tt == 0 else slice(PAST + DEC, PAST + DEC + P * tt)


def width(tt):
    return PAST + DEC if tt == 0 else P * tt


def key_blocks(tt):
    return [(0, P), (P, DEC)] if tt == 0 else [(P * b, P) for b in range(tt)]


PANELS = [("kv", 0), ("kv", 1), ("iq", 0), ("aq", 0), ("aq", 1)]
PANELS += [(k, i) for k, n in (("gq", 2), ("gk", 2), ("gv", 4), ("gr", 4), ("ga", 4), ("gb", 4)) for i in range(n)]
BRANCH0 = len(PANELS)
PANELS += [(k, i) for i in range(4) for k in ("wa", "wb")]
OUT0 = len(PANELS)
PANELS += [("out", i) for i in (0, 1, 2, 3, 0, 1)]
UP0 = len(PANELS)
PANELS += [("up", i) for i in range(KF)]
DOWN0 = len(PANELS)
DK_GROUPS = [(0, KF % 4)] + [(k, 4) for k in range(KF % 4, KF, 4)]
NG = len(DK_GROUPS)
PANELS += [("down", (n, k, c)) for n in range(2) for k, c in DK_GROUPS]
NP = len(PANELS)
FEAT = {"aq": (4, 2), "iq": (2, 2), "gq": (4, 2), "gk": (4, 2), "gr": (8, 2), "ga": (8, 2), "gb": (8, 2)}


class Job:
    def __init__(self, panel, n, k0, kn, tiles, banks, first, last):
        self.panel, self.n, self.k0, self.kn, self.tiles, self.banks = panel, n, k0, kn, tiles, banks
        self.first, self.last = first, last


OUT_JOBS = [Job(OUT0 + i, i // 2, 4 * (i % 2), 4, (0, 1, 2), ((4, 5, 6), (7, 0, 1))[i // 2], i % 2 == 0, i % 2 == 1)
            for i in range(4)]
OUT_JOBS += [Job(OUT0 + 2 + i, 1, 4 * i, 4, (3, 4), (2, 3), i == 0, i == 1) for i in range(2)]
OUT_JOBS += [Job(OUT0 + 4 + i, 0, 4 * i, 4, (3, 4), (4, 5), i == 0, i == 1) for i in range(2)]
DOWN_JOBS = [Job(DOWN0 + n * NG + g, n, k, c, tuple(range(TILES)), tuple((4 + 5 * n + t) % 8 for t in range(TILES)), g == 0, g == NG - 1)
             for n in range(2) for g, (k, c) in enumerate(DK_GROUPS)]
JOBS = OUT_JOBS + DOWN_JOBS


def job_signal(job):
    i = JOBS.index(job)
    if job.last:
        return "wide_done", sum(len(j.tiles) for j in JOBS[:i + 1] if j.last)
    return "panel_used", 1 + sum(not j.last for j in JOBS[:i + 1])


def wide_order(job, t):
    return job_signal(job)[1] - len(job.tiles) + t + 1


def sample_order(job):
    return sum(j.last and 0 in j.tiles for j in JOBS[:JOBS.index(job) + 1])


class Slot:
    def __init__(self, kind, i, part, panel, opens, closes, unit, ends):
        self.kind, self.i, self.part, self.panel = kind, i, part, panel
        self.opens, self.closes, self.unit, self.ends = opens, closes, unit, ends


def plan_slots():
    slots, unit = [], 0

    def blocks(kind, which):
        nonlocal unit
        first = PANELS.index((kind, 0))
        for i in which:
            for j in range(2):
                slots.append(Slot(kind, i, j, first + i // 2, i % 2 == 0 and j == 0, i % 2 == 1 and j == 1, unit, j == 1))
            unit += 1

    def gate_logits(i):
        nonlocal unit
        slots.append(Slot("z", i, 0, None, False, False, unit, True))
        unit += 1

    for kind in ("iq", "aq", "gq", "gk"):
        blocks(kind, range(FEAT[kind][0]))
    for p in range(4):
        for tt in range(TILES):
            ends = tt % 2 == 1 or tt == TILES - 1
            slots.append(Slot("gv", p, tt, PANELS.index(("gv", p)), tt == 0, tt == TILES - 1, unit, ends))
            unit += ends
            if tt == 1:
                gate_logits(p)
    for i in range(8):
        blocks("gr", [i])
    blocks("ga", range(8))
    blocks("gb", range(8))
    return slots, unit


SLOTS, UNITS1 = plan_slots()

IDX_TILES = [0, 2, 3, 4]
ATT_TILES = [1, 0, 2, 3, 4]
NATT = len(ATT_TILES) * QH
GLA_STEPS = [("a", 0), ("b", 0)] + [(s, t) for t in range(1, TILES) for s in "abc"]
AT_IDX, AT_ATT = 5, 13
ATT_ROOM = 1800
ATT_SLOTS = [n for n, s in enumerate(SLOTS) if n >= AT_ATT and s.kind != "z"][:NATT + 4]
AT_GLA = ATT_SLOTS[-1] + 1
AT_NORM = AT_GLA + len(GLA_STEPS) + 2


def plan_aux():
    aux = {}

    def put(s, op):
        aux.setdefault(s, []).append(op)

    put(2, ("keyt", 0))
    for i in range(len(IDX_TILES)):
        put(AT_IDX + i, ("idx", i))
    for n, s in enumerate(ATT_SLOTS):
        put(s, ("att", n))
    for i in range(len(GLA_STEPS)):
        put(AT_GLA + i + (i > 0), ("gla", i))
    put(0, ("coef", 0))
    put(AT_NORM, ("dsplit", 0))
    for h in range(GH):
        put(AT_NORM + 4 * h, ("square", h))
        put(AT_NORM + 4 * h + 1, ("norm", h))
        put(AT_NORM + 4 * h + 2, ("scale", h))
        put(AT_NORM + 4 * h + 4, ("gsplit", h))
    rounds = [(i, r) for i, tt in enumerate(IDX_TILES) for r in range((TOPK_S if tt == 0 else TOPK_P) // 8)]
    s = AT_IDX + 1
    n, room = 0, 0
    while n < len(rounds):
        if SLOTS[s - 1].kind != "z":
            room += 1000 if s < AT_IDX + len(IDX_TILES) else 1600 if s < AT_ATT else ATT_ROOM
        while n < len(rounds) and AT_IDX + rounds[n][0] < s and room > 0:
            put(s, ("topk", rounds[n:n + 1]))
            room -= 2 * width(IDX_TILES[rounds[n][0]]) + 220
            n += 1
        s += 1
        if n:
            j = rounds[n - 1][0]
            assert IDX_TILES[j] not in ATT_TILES or s <= ATT_SLOTS[QH * ATT_TILES.index(IDX_TILES[j])], (s, j)
    for n, s_ in enumerate(SLOTS):
        if s_.kind == "z":
            put(n, ("soft", s_.i))
            put(n + 1, ("scan", s_.i))
            put(n + 2, ("decay", s_.i))
            put(n + 3, ("apply", s_.i))
    assert max(aux) < len(SLOTS), (max(aux), len(SLOTS))
    return aux


AUX = plan_aux()
UNITS2 = UNITS1 + 2 * KD
SECOND_HALF = [next(j.n for j in OUT_JOBS[::-1] if j.last and tt in j.tiles) for tt in range(TILES)]
TURN_BANKS = [(6, 7), (0, 1), (6, 7), (5, 7), (1, 3)]
OUT_PLAN = [("split", OUT0 + 1), ("split", OUT0 + 2), ("evac", 1, 0), ("evac", 1, 1), ("evac", 1, 2), ("split", OUT0 + 3),
            ("evac", 3, 0), ("residual", 0), ("evac", 3, 1), ("residual", 1), ("norm", 0), ("evac", 3, 2), ("residual", 2),
            ("norm", 1), ("split", OUT0 + 4), ("turned", 0), ("split", OUT0 + 5), ("norm", 2), ("evac", 5, 0), ("evac", 5, 1),
            ("turned", 1), ("turned", 2), ("split", UP0), ("evac", 7, 0), ("evac", 7, 1), ("split", UP0 + 1), ("residual", 3),
            ("residual", 4), ("norm", 3), ("norm", 4), ("turned", 3), ("turned", 4)]
TAILS_BANK = 3
Z_UNIT = [s.unit for s in SLOTS if s.kind == "z"]


def layer_kernel(nc, A, O):
    gate_dram = nc.dram_tensor("gate_scratch", (16, P, T), F32, kind="Internal").ap()
    silu_dram = nc.dram_tensor("silu_scratch", (8, P, T), F32, kind="Internal").ap()
    x1_dram = nc.dram_tensor("x1_scratch", (TILES, P, D), F32, kind="Internal").ap()

    with ExitStack() as ctx:
        base = (nc.sbuf_base + 63) // 64 * 64

        def at(name, shape, dtype, offset):
            size = 4
            for d in shape[1:]:
                size *= d
            assert base + offset + size <= nc.sbuf_usable_end, name
            return nc.alloc_sbuf_tensor_at(name, shape, dtype, offset=base + offset)

        def sem(name):
            return ctx.enter_context(nc.semaphore(name))

        ps = ctx.enter_context(nc.psum_tensor("ps", [P, 8, 512], F32))

        raw = at("raw", [P, 2, 2048], F32, 0)
        whi = at("whi", [P, 2, 2048], F32R, 16384)
        wlo = at("wlo", [P, 2, 2048], F32R, 32768)
        xs = at("xs", [P, KD, DEC + 2 * T], F32R, 49152)
        xhi, xlo, xsample = xs[:, :, DEC:DEC + T], xs[:, :, DEC + T:], xs[:, :, 0:2 * DEC]
        o = 88064
        ident = at("ident", [P, P], F32, o)
        ones = at("ones", [P, P], F32, o + 512)
        cmask = at("cmask", [P, GH, P], F32, o + 1024)
        restart = at("restart", [P, T], F32, o + 3072)
        cols = at("cols", [P, 288], F32, o + 5376)
        small = at("small", [P, 128], F32, o + 6528)
        ebl = at("ebl", [P, GH, NCH], F32, o + 7040)
        iws = at("iws", [P, TILES, IH], F32, o + 7200)
        convs = at("convs", [P, 4, 2 * KF], F32, o + 7296)
        o = 88064 + 8064
        v_tok = at("v_tok", [P, TILES, D], F32, o)
        x_tok = at("x_tok", [P, TILES, D], F32, o)
        ghi = at("ghi", [P, KD, T], F32R, o)
        qk = at("qk", [P, 2 * GH, T], F32, o + 20480)
        gq, gk, got = qk[:, 0:GH, :], qk[:, GH:2 * GH, :], qk
        gates_in = at("gates_in", [P, 4, T], F32, o + 20480)
        gpost = at("gpost", [P, D], F32, o + 20480 + 9216)
        gffn = at("gffn", [P, D], F32, o + 20480 + 9216 + 4096)
        o1 = o + 38912
        iz = at("iz", [P, 2, PAST + T], F32, o1)
        iqt = at("iqt", [P, 2, T], F32, o1 + 5632)
        krem = at("krem", [P, GH, T], F32, o1)
        kz = at("kz", [P, 2, PAST + T], F32, o1 + 10240)
        kvi = at("kvi", [P, TILES, 404], F32, o1 + 15872)
        cache = at("cache", [P, 3, P], F32, o1 + 23968)
        glow = at("glow", [P, T], F32, o1 + 25504)
        wgu = at("wgu", [P, GH * DK], F32, o1 + 27808)
        glo = at("glo", [P, KD, T], F32R, o1)
        dhi = at("dhi", [P, 4, T], F32R, o1 + 18432)
        x_re = at("x_re", [P, TILES, D], F32, o1)
        o2 = o1 + 29856
        aqt = at("aqt", [P, 4, T], F32, o2)
        state = at("state", [P, 2, GH, DV], F32, o2 + 9216)
        tmp = at("tmp", [P, 3, T], F32, o2 + 17408)
        stage = at("stage", [P, 2, T], F32, o2 + 24320)
        gpre = at("gpre", [P, D], F32, o2 + 24320)
        junk = at("junk", [P, D], F32, o2 + 17408)
        o3 = o2 + 28928
        score = [at(f"score{i}", [P, width(tt)], F32, o3 + off)
                 for i, (tt, off) in enumerate(zip(IDX_TILES, (0, 768, 1792, 3328)))]
        bias0 = at("bias0", [P, P], F32, o3 + 5376)
        lg = at("lg", [P, 3, 512], F32, o3 + 5888)
        pt = at("pt", [P, 2, 512], F32, o3 + 12032)
        otok = at("otok", [P, QH * HD], F32, o3 + 16128)
        relus = at("relus", [P, IH, 512], F32, o3 + 5888)
        coef_rows = at("coef_rows", [P, 3, P], F32, o3)
        scm = at("scm", [P, GH, P], F32, o3)
        krem_a = at("krem_a", [P, GH, P], F32, o3 + 2048)
        krem_b = at("krem_b", [P, GH, P], F32, o3 + 4096)
        qa = at("qa", [P, GH, P], F32, o3 + 6144)
        qb = at("qb", [P, GH, P], F32, o3 + 8192)
        dlo = at("dlo", [P, 4, T], F32R, o3)
        silu_in = at("silu_in", [P, 2, T], F32, o3 + 10240)
        y_tok = at("y_tok", [P, TILES, D], F32, o)
        xn_tok = at("xn_tok", [P, 2, D], F32, o3)
        us = at("us", [P, KF, DEC + UW + SEQ], F32R, o)
        uhi, ulo, usample = us[:, :, DEC:DEC + UW], us[:, :, DEC + UW:], us[:, :, 0:2 * DEC]
        o4 = o + 2 * 50880
        ha = at("ha", [P, 2, CU], F32, o4)
        hb = at("hb", [P, 2, CU], F32, o4 + 4640)
        ca = at("ca", [P, CU], F32, o4 + 9280)
        cb = at("cb", [P, UW], F32, o4 + 11616)
        conv_rows = at("conv_rows", [P, 2, P], F32, 49152 + 32768)
        y2_tok = at("y2_tok", [P, TILES, D], F32, 49152)
        x1_in = at("x1_in", [P, 2, D], F32, 49152 + 20480)
        x1_more = at("x1_more", [P, 2, D], F32, o4 + 4640)
        x1_back = [x1_in[:, 0, :], x1_in[:, 1, :], x1_more[:, 0, :], x1_more[:, 1, :]]
        gfin = at("gfin", [P, D], F32, 49152 + 28672)
        junk2 = at("junk2", [P, D], F32, o4)

        ssq, rstd = small[:, 0:5], small[:, 16:21]
        negmax, rowsum, rinv = small[:, 24:27], small[:, 28:32], small[:, 32:34]
        m8, gnh = small[:, 40:48], small[:, 50:52]
        wsq, wsum, wfirst, eps = small[:, 56:66], small[:, 68:73], small[:, 76:81], small[:, 84:85]
        table_probe = small[:, 88:89]
        col_gate, col_hn = cols[:, 88:92], cols[:, 92:94]
        cw0, cw1, cw2, cbias = cols[:, 0:44], cols[:, 44:88], cols[:, 96:140], cols[:, 140:184]
        cstate = cols[:, 184:272]

        x_loaded = [sem(f"x_loaded{tt}") for tt in range(TILES)]
        gpre_loaded, coefs_loaded, cache_loaded = sem("gpre_loaded"), sem("coefs_loaded"), sem("cache_loaded")
        state_loaded = sem("state_loaded")
        raw_loaded = [sem("raw_loaded0"), sem("raw_loaded1")]
        hi_ready, lo_ready, panel_used = sem("hi_ready"), sem("lo_ready"), sem("panel_used")
        act_chain, dve_chain, pool_chain = sem("act_chain"), sem("dve_chain"), sem("pool_chain")
        consts_ready = sem("consts_ready")
        coefs_turned, coefs_ready = sem("coefs_turned"), sem("coefs_ready")
        stats_primed = sem("stats_primed")
        sumsq_ready, root_ready, xn_ready = sem("sumsq_ready"), sem("root_ready"), sem("xn_ready")
        x_turned, xhi_ready, xlo_ready = sem("x_turned"), sem("xhi_ready"), sem("xlo_ready")
        kv_done, kv_copied, keys_turned, keys_ready = sem("kv_done"), sem("kv_copied"), sem("keys_turned"), sem("keys_ready")
        unit_done, unit_free = sem("unit_done"), [sem("unit_free0"), sem("unit_free1")]
        tanh_ready, stage_saved = sem("tanh_ready"), [sem("stage_saved0"), sem("stage_saved1")]
        dots_done, relu_ready, scored = sem("dots_done"), sem("relu_ready"), sem("scored")
        logits_done, masked, probs_ready = sem("logits_done"), sem("masked"), sem("probs_ready")
        probs_turned, pt_ready, pv_done, o_scaled = sem("probs_turned"), sem("pt_ready"), sem("pv_done"), sem("o_scaled")
        o_turned, o_ready = sem("o_turned"), sem("o_ready")
        soft_ready, diff_ready = sem("soft_ready"), sem("diff_ready")
        decay_exp, decay_used = sem("decay_exp"), sem("decay_used")
        gla_a, gla_b, gla_c = sem("gla_scores_done"), sem("gla_chunk_a_done"), sem("gla_chunk_b_done")
        pads_zero, q_padded, krem_ready, sc_masked, state_ready, got_copied = (
            sem("pads_zero"), sem("q_padded"), sem("krem_ready"), sem("sc_masked"), sem("state_ready"), sem("got_copied"))
        sq_ready, norm_summed, head_root, head_out = (
            sem("sq_ready"), sem("norm_summed"), sem("head_root"), sem("head_out"))
        silu_loaded, ghi_ready, glo_ready, dhi_ready, dlo_ready = (
            sem("silu_loaded"), sem("ghi_ready"), sem("glo_ready"), sem("dhi_ready"), sem("dlo_ready"))
        gates_loaded = [sem("gates_loaded0"), sem("gates_loaded1")]
        merged, mhi_ready, mlo_ready = sem("merged"), sem("mhi_ready"), sem("mlo_ready")
        posts_loaded, x_reloaded = sem("posts_loaded"), sem("x_reloaded")
        wide_done, wide_squared, wide_free, first_half, yroot_ready, x1_ready = (
            sem("wide_done"), sem("wide_squared"), sem("wide_free"), sem("first_half"), sem("yroot_ready"), sem("x1_ready"))
        x1_sq, xroot_ready, xn2_ready = sem("x1_sq"), sem("xroot_ready"), sem("xn2_ready")
        x2_turned, x2hi_ready, x2lo_ready, x1_saved = sem("x2_turned"), sem("x2hi_ready"), sem("x2lo_ready"), sem("x1_saved")
        h_ready, rim_ready, taps_done, ca_ready, gelu_ready, u_ready, uhi_ready, ulo_ready, tails_saved = (
            sem("h_ready"), sem("rim_ready"), sem("taps_done"), sem("ca_ready"), sem("gelu_ready"), sem("u_ready"), sem("uhi_ready"), sem("ulo_ready"), sem("tails_saved"))
        tails_turned, tails_ready, gfin_loaded = sem("tails_turned"), sem("tails_ready"), sem("gfin_loaded")
        x1_loaded = [sem(f"x1_loaded{b}") for b in range(4)]
        tables_in, sample_low, sample_summed = sem("tables_in"), sem("sample_low"), sem("sample_summed")
        out_ready, stored, y_stored = sem("out_ready"), sem("stored"), sem("y_stored")

        w_in, w_up, w_down = A["w_in"][0], A["w_up"][0], A["w_down"][0]

        def cols_of(w, c0, n, k0=0, k=KD):
            return w[k0 * P:(k0 + k) * P, c0:c0 + n].rearrange("(k p) c -> p k c", p=P)

        def up_loads(j, r):
            d = raw[:, r, :].rearrange("p (k n) -> p k n", k=KD)
            return [(d[:, :, P * g:P * g + P],
                     w_up[:, bass.ds(j * P + FFN * g, P)].rearrange("(k p) c -> p k c", p=P)) for g in range(2)]

        def panel_loads(p):
            kind, i = PANELS[p]
            slot = raw[:, p % 2, :]

            def dst(k, n):
                return slot[:, 0:k * n].rearrange("p (k n) -> p k n", k=k)
            if kind == "kv":
                d = dst(4, 340)
                return [(d[:, :, 0:256], cols_of(w_in, O_AK, 256, 4 * i, 4)),
                        (d[:, :, 256:324], cols_of(w_in, O_IK, ID + IH, 4 * i, 4)),
                        (d[:, :, 324:340], cols_of(w_in, O_LOW, RANK, 4 * i, 4))]
            if kind == "aq":
                d = dst(KD, 256)
                return [(d[:, :, b * 128 + half * 64:b * 128 + half * 64 + 64],
                         cols_of(w_in, O_AQ + (2 * i + b + 4 * half) * HD, HD)) for b in range(2) for half in range(2)]
            simple = {"iq": O_IQ, "gq": O_GQ, "gk": O_GK, "gv": O_GV, "gr": O_GR, "ga": O_GATE, "gb": O_GATE + D}
            if kind in simple:
                return [(dst(KD, 256), cols_of(w_in, simple[kind] + 256 * i, 256))]
            if kind == "wa":
                return [(dst(KD, 256), cols_of(A["w_branch_gla"][0], 256 * i, 256))]
            if kind == "wb":
                return [(dst(4, 256), cols_of(A["w_branch_dsa"][0], 256 * i, 256, 0, 4))]
            if kind == "out":
                return [(dst(4, 512), cols_of(A["w_out"][0], 512 * (i // 2), 512, 4 * (i % 2), 4))]
            if kind == "up":
                return up_loads(i, p % 2)
            n, k, c = i
            return [(dst(c, 512), cols_of(w_down, 512 * n, 512, k, c))]

        def panel_size(p):
            kind, i = PANELS[p]
            return {"kv": 1360, "wb": 1024, "down": 512 * i[2] if kind == "down" else 0}.get(kind, 2048)

        def loaded(p):
            return 16 * sum(len(panel_loads(q)) for q in range(p % 2, p + 1, 2))

        def branch_ring(g):
            return (BRANCH0 + g) % 2, panel_size(BRANCH0 + g)

        def branch_loaded(q, g):
            return loaded(BRANCH0 + g) + 16 * q

        def up_slot(r):
            return (UP0 + r) % 2

        def up_loaded(i, r):
            return loaded(UP0 + r) + 32 * i

        def wait_panel_used(eng, p):
            kind, i = PANELS[p]
            if kind == "kv":
                eng.wait_ge(*((panel_used, 1) if i == 0 else (kv_done, TILES)))
            elif p < BRANCH0:
                eng.wait_ge(unit_done, 1 + max(s.unit for s in SLOTS if s.panel == p))
            elif p < OUT0:
                eng.wait_ge(unit_done, UNITS1 + 2 * (p - BRANCH0) + 2)
            elif UP0 <= p < DOWN0:
                eng.wait_ge(unit_done, UNITS2 + 2 * (p - UP0 + 1))
            else:
                name, value = job_signal([j for j in JOBS if j.panel == p][-1])
                eng.wait_ge({"wide_done": wide_done, "panel_used": panel_used}[name], value)

        def unit_waits(eng, unit):
            if unit >= 2:
                eng.wait_ge(unit_free[unit % 2], unit // 2)

        block = ctx.enter_context(nc.Block())

        def store_result(eng, tt):
            eng.wait_ge(out_ready, tt + 1)
            dst = O["y_s"][0] if tt == 0 else O["y_p"][0, P * (tt - 1):P * tt, :]
            eng.dma_start(dst, y2_tok[0:rows(tt), tt, :]).then_inc(y_stored, 16)

        @block.sync
        def _(sp):
            def load_x(tt):
                src = A["x_sample"][0] if tt == 0 else A["x_prompt"][0, P * (tt - 1):P * tt, :]
                sp.dma_start(x_tok[0:rows(tt), tt, :], src).then_inc(x_loaded[tt], 16)

            def load(p):
                if p >= 2:
                    sp.wait_ge(lo_ready, p - 1)
                for d, s in panel_loads(p):
                    sp.dma_start(d, s).then_inc(raw_loaded[p % 2], 16)

            load_x(0)
            sp.dma_start(gpre[:, :], A["attn_pre_norm"][0].partition_broadcast(P)).then_inc(gpre_loaded, 16)
            load_x(1)
            for p in range(UP0 + 2):
                load(p)
                if p == 0:
                    for tt in range(2, TILES):
                        load_x(tt)
                if p == 1:
                    ck, cv = A["cache_k"][0, 0], A["cache_v"][0, 0]
                    sp.dma_start(cache[:, 0, :], ck.rearrange("s g d -> s (g d)")).then_inc(cache_loaded, 16)
                    sp.dma_start(cache[:, 1, :], cv.rearrange("s g d -> s (g d)")).then_inc(cache_loaded, 16)
                    for half in range(2):
                        sp.dma_start(cache[:, 2, half * 64:half * 64 + 64], A["cache_k_idx"][0, 0]).then_inc(cache_loaded, 16)
                    sp.wait_ge(pads_zero, 1)
                    sp.dma_start(wgu[0:RANK, :], A["w_gla_gate_up"][0]).then_inc(state_loaded, 16)
                    sp.dma_start(state[:, 0, :, :], A["state_gla"][0, 0].rearrange("h d v -> d h v")).then_inc(state_loaded, 16)
            with sp.Fori(1, KF // 2) as i:
                for r in range(2):
                    j = 2 * i + r
                    sp.wait_ge(lo_ready, UP0 + j - 1)
                    for d, s in up_loads(j, up_slot(r)):
                        sp.dma_start(d, s).then_inc(raw_loaded[up_slot(r)], 16)
            for p in range(DOWN0, NP):
                load(p)
            sp.wait_ge(x1_saved, 16 * TILES)
            sp.wait_ge(h_ready, 2 * KF)
            for tt in range(TILES):
                if tt == 2:
                    sp.wait_ge(ulo_ready, KF)
                    sp.wait_ge(tails_saved, 4 * KF)
                if tt == TILES - 1:
                    sp.wait_ge(out_ready, 1)
                sp.dma_start(x1_back[tt % 4][0:rows(tt), :], x1_dram[tt, 0:rows(tt)]).then_inc(x1_loaded[tt % 4], 16)
            for tt in range(TILES - 2):
                store_result(sp, tt)
            store_result(sp, TILES - 2)
            store_result(sp, TILES - 1)
            sp.wait_ge(y_stored, 16 * TILES)
            sp.wait_ge(stored, 16 * (8 + 2))

        @block.gpsimd
        def _(pool):
            chain = [0]

            def link(ins):
                chain[0] += 1
                ins.then_inc(pool_chain, 1)
                pool.wait_ge(pool_chain, chain[0])

            cwt = A["conv_w"][0].rearrange("j (b p) -> j b p", p=P)
            cst = A["state_ffn_conv"][0, 0].rearrange("j (b p) -> j b p", p=P)
            nb = 2 * KF
            link(nc.gpsimd.memset(ident[:, :], 0.0))
            nc.gpsimd.affine_select(out=ident[:, :], in_=ident[:, :], compare_op=ALU.not_equal, fill=1.0, base=0,
                                    pattern=[[-1, P]], channel_multiplier=1).then_inc(consts_ready, 1)
            for r, n, t, src in ((0, nb, 0, cwt[0]), (nb, nb, 0, cwt[1]),
                                 (2 * nb, 4, 0, A["b_gla_gate"][0].rearrange("(b p) -> b p", p=P)),
                                 (2 * nb + 4, 2, 0, A["gla_head_norm"].rearrange("l (b p) -> (l b) p", p=P)),
                                 (0, nb, 1, cwt[2]), (nb, nb, 1, A["conv_b"][0].rearrange("(b p) -> b p", p=P)),
                                 (0, nb, 2, cst[0]), (nb, nb, 2, cst[1])):
                pool.dma_start(coef_rows[r:r + n, t, :], src).then_inc(coefs_loaded, 16)
            nc.gpsimd.memset(ones[:, :], 1.0).then_inc(consts_ready, 1)
            link(nc.gpsimd.memset(cmask[:, :, :], 1.0))
            link(nc.gpsimd.affine_select(out=cmask[:, :, :], in_=cmask[:, :, :], compare_op=ALU.is_ge, fill=0.0, base=0,
                                         pattern=[[0, GH], [1, P]], channel_multiplier=-1))
            nc.gpsimd.memset(cmask[0:CHUNK, :, CHUNK:P], 0.0).then_inc(consts_ready, 1)
            link(nc.gpsimd.memset(restart[:, :], 1.0))
            nc.gpsimd.memset(restart[:, :].rearrange("p (n c) -> p n c", c=CHUNK)[:, :, 0:1], 0.0).then_inc(consts_ready, 1)
            nc.gpsimd.memset(wgu[:, :], 0.0).then_inc(pads_zero, 1)
            nc.gpsimd.memset(glow[:, :], 0.0).then_inc(pads_zero, 1)
            nc.gpsimd.memset(kz[:, :, :], 0.0).then_inc(pads_zero, 1)
            nc.gpsimd.memset(iz[:, :, :], 0.0).then_inc(pads_zero, 1)
            nc.gpsimd.memset(state[:, 1, :, :], 0.0).then_inc(pads_zero, 1)
            pool.wait_ge(coefs_turned, 1)
            link(nc.gpsimd.memset(bias0[:, :], 0.0))
            nc.gpsimd.memset(bias0[0:CHUNK, CHUNK:P], -BIG).then_inc(pads_zero, 1)

            pool.wait_ge(kv_copied, TILES)
            kp, vp, ip = (O[n][0, 0].rearrange("(t p) g d -> p t (g d)", p=P) if n != "kidx_p" else
                          O[n][0, 0].rearrange("(t p) d -> p t d", p=P) for n in ("k_p", "v_p", "kidx_p"))
            pool.dma_start(kp, kvi[:, 1:TILES, 0:128]).then_inc(stored, 16)
            pool.dma_start(vp, kvi[:, 1:TILES, 128:256]).then_inc(stored, 16)
            pool.dma_start(ip, kvi[:, 1:TILES, 256:320]).then_inc(stored, 16)
            pool.dma_start(O["k_s"][0, 0].rearrange("s g d -> s (g d)"), kvi[0:DEC, 0, 0:128]).then_inc(stored, 16)
            pool.dma_start(O["v_s"][0, 0].rearrange("s g d -> s (g d)"), kvi[0:DEC, 0, 128:256]).then_inc(stored, 16)
            pool.dma_start(O["kidx_s"][0, 0], kvi[0:DEC, 0, 256:320]).then_inc(stored, 16)

            staged = 0
            for s, slot in enumerate(SLOTS):
                if slot.kind in ("gr", "ga", "gb") and slot.ends:
                    pool.wait_ge(unit_free[slot.unit % 2], slot.unit // 2 + 1)
                    dst = silu_dram[slot.i] if slot.kind == "gr" else gate_dram[slot.i + (8 if slot.kind == "gb" else 0)]
                    pool.dma_start(dst, stage[:, staged % 2, :]).then_inc(stage_saved[staged % 2], 16)
                    staged += 1
                for op, n in AUX.get(s, []):
                    if op == "gla":
                        step, tt = GLA_STEPS[n]
                        if n == 0:
                            pool.wait_ge(o_ready, len(ATT_TILES))
                            for b in (scm, krem_a, krem_b, qa[:, :, CHUNK:P], qb[:, :, 0:CHUNK]):
                                nc.gpsimd.memset(b[:, :, :], 0.0).then_inc(pads_zero, 1)
                            pool.wait_ge(pads_zero, 11)
                            pool.wait_ge(decay_used, 3 * GH)
                        if step == "a":
                            if tt >= 1:
                                pool.wait_ge(gla_b, tt)
                            if tt >= 2:
                                pool.wait_ge(gla_c, tt - 1)
                            c0 = tok(tt).start
                            nc.gpsimd.tensor_copy(qa[:, :, 0:CHUNK], gq[:, :, c0:c0 + CHUNK]).then_inc(q_padded, 1)
                            nc.gpsimd.tensor_copy(qb[:, :, CHUNK:P], gq[:, :, c0 + CHUNK:c0 + P]).then_inc(q_padded, 1)
                    if op == "square":
                        pool.wait_ge(gla_c, TILES - 1)
                        if n == 0:
                            pool.wait_ge(stage_saved[0], 16 * 4)
                            pool.wait_ge(stage_saved[1], 16 * 4)
                        else:
                            pool.wait_ge(head_out, n)
                        pool.dma_start(silu_in[:, :, :], silu_dram[2 * n:2 * n + 2].rearrange("b p t -> p b t"))\
                            .then_inc(silu_loaded, 16)
            pool.wait_ge(state_ready, 2 * TILES - 1)
            pool.dma_start(O["gla_s"][0, 0].rearrange("h d v -> d h v"), state[:, 0, :, :]).then_inc(stored, 16)
            pool.dma_start(O["gla_p"][0, 0].rearrange("h d v -> d h v"), state[:, 1, :, :]).then_inc(stored, 16)
            pool.wait_ge(stage_saved[0], 16 * 12)
            pool.wait_ge(stage_saved[1], 16 * 12)
            pool.wait_ge(glo_ready, GH)
            for q in range(KD):
                m, g = 2 * (q // 2), q % 2
                if q >= 2:
                    for u in (UNITS1 + 2 * q - 4, UNITS1 + 2 * q - 3):
                        pool.wait_ge(unit_free[u % 2], u // 2 + 1)
                pool.dma_start(gates_in[:, 2 * g:2 * g + 2, :], gate_dram[8 * g + m:8 * g + m + 2].rearrange("b p t -> p b t"))\
                    .then_inc(gates_loaded[g], 16)
                if q == 0:
                    pool.dma_start(gpost[:, :], A["attn_post_norm"][0].partition_broadcast(P)).then_inc(posts_loaded, 16)
                    pool.dma_start(gffn[:, :], A["ffn_pre_norm"][0].partition_broadcast(P)).then_inc(posts_loaded, 16)
            wait_panel_used(pool, OUT0 - 1)
            pool.wait_ge(stored, 16 * 8)
            for tt in range(TILES):
                src = A["x_sample"][0] if tt == 0 else A["x_prompt"][0, P * (tt - 1):P * tt, :]
                pool.dma_start(x_re[0:rows(tt), tt, :], src).then_inc(x_reloaded, 16)
            for tt in range(TILES):
                pool.wait_ge(x1_ready, tt + 1)
                pool.dma_start(x1_dram[tt, 0:rows(tt)], x_re[0:rows(tt), tt, :]).then_inc(x1_saved, 16)
            pool.wait_ge(x2lo_ready, 2 * TILES)
            for i in range(2):
                for h in (ha, hb):
                    nc.gpsimd.memset(h[:, i, 2 + DEC:4 + DEC], 0.0).then_inc(pads_zero, 1)

            def rims_and_tails(i, r, first=False):
                j = 2 * i + r
                for g, h in enumerate((ha, hb)):
                    if not first:
                        pool.wait_ge(ca_ready, 2 * j + g - 3)
                    rim = cstate.rearrange("p (i b) -> p i b", i=2)[:, :, bass.ds(j + KF * g, 1)]
                    nc.gpsimd.tensor_copy(h[:, r, 0:2].rearrange("p (i b) -> p i b", i=2), rim).then_inc(rim_ready, 1)
                for g, h in enumerate((ha, hb)):
                    pool.wait_ge(h_ready, 2 * j + g + 1)
                    for t, end in enumerate((2 + DEC, CU)):
                        nc.gpsimd.tensor_copy(convs[:, 2 * t:2 * t + 2, bass.ds(j + KF * g, 1)],
                                              h[:, r, end - 2:end].rearrange("p (i b) -> p i b", i=2)).then_inc(tails_saved, 1)

            for r in range(2):
                rims_and_tails(0, r, True)
            with pool.Fori(1, KF // 2) as i:
                for r in range(2):
                    rims_and_tails(i, r)
            pool.dma_start(gfin[:, :], A["ffn_post_norm"][0].partition_broadcast(P)).then_inc(gfin_loaded, 16)
            pool.wait_ge(tails_ready, 1)
            pool.dma_start(O["conv_s"][0, 0].rearrange("j (b p) -> (j b) p", p=P), conv_rows[0:2 * nb, 0, :]).then_inc(stored, 16)
            pool.dma_start(O["conv_p"][0, 0].rearrange("j (b p) -> (j b) p", p=P), conv_rows[0:2 * nb, 1, :]).then_inc(stored, 16)

        @block.scalar
        def _(act):
            chain = [0]

            def link(ins):
                chain[0] += 1
                ins.then_inc(act_chain, 1)
                act.wait_ge(act_chain, chain[0])

            def split(p):
                if p >= NP:
                    return
                act.wait_ge(raw_loaded[p % 2], loaded(p))
                if p >= 2:
                    wait_panel_used(act, p - 2)
                n = panel_size(p)
                nc.scalar.activation(whi[:, p % 2, 0:n], raw[:, p % 2, 0:n], ACT.Copy).then_inc(hi_ready, 1)

            def feat(ap):
                return ap.rearrange("p (a b) -> p a b", a=2)

            def preload_sqrt():
                nc.scalar.activation(table_probe, eps, ACT.Sqrt).then_inc(tables_in, 1)

            act.wait_ge(stats_primed, 2)
            preload_sqrt()

            def square(tt):
                act.wait_ge(x_loaded[tt], 16)
                nc.scalar.activation(junk[0:rows(tt), :], x_tok[0:rows(tt), tt, :], ACT.Square,
                                     accum_out=ssq[0:rows(tt), tt:tt + 1]).then_inc(sumsq_ready, 1)
                act.wait_ge(sumsq_ready, tt + 1)

            def root(tt):
                nc.scalar.activation(rstd[:, tt:tt + 1], ssq[:, tt:tt + 1], ACT.Sqrt, scale=1.0 / D, bias=eps).then_inc(root_ready, 1)

            def turned(tt):
                for kh in range(2):
                    t = 2 * tt + kh
                    act.wait_ge(x_turned, t + 1)
                    n = rows(tt)
                    nc.scalar.activation(xhi[:, 4 * kh:4 * kh + 4, tok(tt).start:tok(tt).start + n],
                                         ps[:, 5 + t % 3, :].rearrange("p (k c) -> p k c", k=4)[:, :, 0:n], ACT.Copy).then_inc(xhi_ready, 1)

            square(0)
            root(0)
            for tt in range(1, TILES):
                square(tt)
                root(tt)
                turned(tt - 1)
                if tt == 1:
                    split(0)
            turned(TILES - 1)
            split(1)
            split(2)
            for tt in range(TILES):
                act.wait_ge(kv_done, tt + 1)
                nc.scalar.activation(kvi[:, tt, 0:320], ps[:, tt, 0:320], ACT.Copy)
                nc.scalar.activation(kvi[:, tt, 320:384], ps[:, tt, 256:320], ACT.Copy)
                nc.scalar.activation(kvi[:, tt, 384:404], ps[:, tt, 320:340], ACT.Copy).then_inc(kv_copied, 1)

            def copy_unit(slot):
                u, i = slot.unit, slot.i
                pair = 2 * (u % 2)
                src = ps[:, pair:pair + 2, 0:HALF]
                free = unit_free[u % 2]
                act.wait_ge(unit_done, u + 1)
                if slot.kind == "aq":
                    nc.scalar.activation(feat(aqt[:, i, :]), src, ACT.Copy).then_inc(free, 1)
                elif slot.kind == "iq":
                    nc.scalar.activation(feat(iqt[:, i, :]), src, ACT.Copy).then_inc(free, 1)
                elif slot.kind == "gq":
                    nc.scalar.activation(feat(gq[:, i, :]), src, ACT.Copy, scale=DK ** -0.5).then_inc(free, 1)
                elif slot.kind == "gk":
                    nc.scalar.activation(feat(gk[:, i, :]), src, ACT.Copy).then_inc(free, 1)
                elif slot.kind == "gv":
                    t0 = slot.part // 2 * 2
                    n = slot.part - t0 + 1
                    nc.scalar.activation(v_tok[:, t0:t0 + n, 256 * i:256 * i + 256], ps[:, pair:pair + n, 0:256],
                                         ACT.Copy).then_inc(free, 1)
                elif slot.kind == "z":
                    if i >= 1:
                        act.wait_ge(decay_used, 3 * i)
                    nc.scalar.activation(feat(tmp[:, 0, :]), src, ACT.Identity, bias=col_gate[:, i:i + 1]).then_inc(free, 1)
                else:
                    n = {"gr": 0, "ga": 8, "gb": 16}[slot.kind] + i
                    if n >= 2:
                        act.wait_ge(stage_saved[n % 2], 16 * (n // 2))
                    nc.scalar.activation(feat(stage[:, n % 2, :]), src, ACT.Tanh, scale=0.5)\
                        .then_inc(tanh_ready if slot.kind == "gr" else free, 1)

            def aux(op, n):
                if op == "coef":
                    act.wait_ge(coefs_turned, 1)
                    nc.scalar.activation(cols[:, 0:94], ps[:, 7, 0:94], ACT.Copy)
                    nc.scalar.activation(cols[:, 96:272], ps[:, 7, 96:272], ACT.Copy).then_inc(coefs_ready, 1)
                elif op == "keyt":
                    act.wait_ge(keys_turned, 1)
                    act.wait_ge(pads_zero, 4)
                    for g in range(2):
                        r = slice(64 * g, 64 * g + 64)
                        nc.scalar.activation(kz[r, g, PAST + DEC:], ps[r, 5, :], ACT.Copy)
                        nc.scalar.activation(iz[r, g, PAST + DEC:], ps[r, 6, :], ACT.Copy)
                        nc.scalar.activation(kz[r, g, 0:PAST + DEC], ps[r, 7, 0:PAST + DEC], ACT.Copy)
                        nc.scalar.activation(iz[r, g, 0:PAST + DEC], ps[r, 7, PAST + DEC:2 * (PAST + DEC)], ACT.Copy)
                    nc.scalar.activation(glow[0:RANK, DEC:T], ps[0:RANK, 4, :], ACT.Copy)
                    nc.scalar.activation(glow[0:RANK, 0:DEC], ps[0:RANK, 7, 384:448], ACT.Copy).then_inc(keys_ready, 1)
                elif op == "idx":
                    w = width(IDX_TILES[n])
                    act.wait_ge(dots_done, n + 1)
                    if n >= 1:
                        act.wait_ge(scored, n)
                    for h in range(IH):
                        nc.scalar.activation(relus[:, h, 0:w], ps[:, 4 + h, 0:w], ACT.Relu).then_inc(relu_ready, 1)
                elif op == "att":
                    if n < NATT:
                        w = width(ATT_TILES[n // QH])
                        act.wait_ge(masked, n + 1)
                        nc.scalar.activation(lg[:, n % 3, 0:w], lg[:, n % 3, 0:w], ACT.Exp, bias=negmax[:, n % 3:n % 3 + 1],
                                             scale=-1.0, accum_out=rowsum[:, n % 4:n % 4 + 1]).then_inc(probs_ready, 1)
                    m = n - 2
                    if 0 <= m < NATT:
                        tt = ATT_TILES[m // QH]
                        act.wait_ge(probs_turned, m + 1)
                        if m >= 2:
                            act.wait_ge(pv_done, m - 1)
                        if tt == 0:
                            nc.scalar.activation(pt[:, m % 2, 0:P], ps[:, 6, 0:P], ACT.Copy)
                            ins = nc.scalar.activation(pt[0:DEC, m % 2, P:2 * P], ps[0:DEC, 6, P:2 * P], ACT.Copy)
                        else:
                            ins = nc.scalar.activation(pt[:, m % 2, 0:P * tt], ps[:, 6, 0:P * tt], ACT.Copy)
                        ins.then_inc(pt_ready, 1)
                    m = n - 4
                    if m >= 0 and m % QH == QH - 1:
                        t = m // QH
                        tt = ATT_TILES[t]
                        act.wait_ge(o_turned, t + 1)
                        k = rows(tt)
                        nc.scalar.activation(aqt[:, :, tok(tt).start:tok(tt).start + k],
                                             ps[:, 4 + (n + 1) % 2, :].rearrange("p (b c) -> p b c", b=4)[:, :, 0:k], ACT.Copy).then_inc(o_ready, 1)
                elif op == "soft":
                    z, a, b = tmp[:, 0, :], tmp[:, 1, :], tmp[:, 2, :]
                    act.wait_ge(unit_free[Z_UNIT[n] % 2], Z_UNIT[n] // 2 + 1)
                    link(nc.scalar.activation(a, z, ACT.Abs))
                    link(nc.scalar.activation(a, a, ACT.Exp, scale=-1.0))
                    nc.scalar.activation(a, a, ACT.Ln, bias=1.0).then_inc(soft_ready, 1)
                elif op == "decay":
                    z, a, b = tmp[:, 0, :], tmp[:, 1, :], tmp[:, 2, :]
                    act.wait_ge(diff_ready, n + 1)
                    nc.scalar.activation(b, b, ACT.Exp, scale=1.0 / TAU).then_inc(decay_exp, 1)
                    nc.scalar.activation(z, a, ACT.Exp, scale=1.0 / TAU).then_inc(decay_exp, 1)
                    link(nc.scalar.activation(ebl[:, n, :], a.rearrange("p (n c) -> p n c", c=CHUNK)[:, :, CHUNK - 1],
                                              ACT.Exp, scale=1.0 / TAU))
                    act.wait_ge(decay_exp, 3 * n + 2)
                    nc.scalar.activation(a, a, ACT.Exp, scale=-1.0 / TAU).then_inc(decay_exp, 1)
                elif op == "gla":
                    step, tt = GLA_STEPS[n]
                    if step == "a":
                        act.wait_ge(gla_a, tt + 1)
                        act.wait_ge(pads_zero, 11)
                        nc.scalar.activation(krem_a[0:CHUNK, :, :], ps[0:CHUNK, 4, :].rearrange("p (h d) -> p h d", h=GH), ACT.Copy)\
                            .then_inc(krem_ready, 1)
                        nc.scalar.activation(krem_b[CHUNK:P, :, :], ps[CHUNK:P, 4, :].rearrange("p (h d) -> p h d", h=GH), ACT.Copy)\
                            .then_inc(krem_ready, 1)
                    elif step == "c" or tt == 0:
                        if tt == 0:
                            act.wait_ge(gla_b, 1)
                        else:
                            act.wait_ge(gla_c, tt)
                        k = rows(tt)
                        nc.scalar.activation(got[:, :, tok(tt).start:tok(tt).start + k],
                                             ps[:, 6:8, :].rearrange("p a (b c) -> p (a b) c", b=4)[:, :, 0:k], ACT.Copy)\
                            .then_inc(got_copied, 1)
                elif op == "square":
                    if n >= 1:
                        act.wait_ge(norm_summed, n)
                    act.wait_ge(got_copied, TILES)
                    nc.scalar.activation(tmp[:, 0:2, :], got[:, 2 * n:2 * n + 2, :], ACT.Square).then_inc(sq_ready, 1)
                elif op == "norm":
                    act.wait_ge(norm_summed, n + 1)
                    if n >= 1:
                        act.wait_ge(head_out, n)
                    nc.scalar.activation(feat(tmp[:, 2, :]), ps[:, 4:6, 0:HALF], ACT.Sqrt, scale=1.0 / DV, bias=eps)\
                        .then_inc(head_root, 1)
                elif op == "gsplit":
                    act.wait_ge(head_out, n + 1)
                    nc.scalar.activation(ghi[:, 2 * n:2 * n + 2, :], got[:, 2 * n:2 * n + 2, :], ACT.Copy).then_inc(ghi_ready, 1)
                elif op == "dsplit":
                    act.wait_ge(stored, 16 * 6)
                    nc.scalar.activation(dhi[:, :, :], aqt[:, :, :], ACT.Copy).then_inc(dhi_ready, 1)

            for s, slot in enumerate(SLOTS):
                if slot.ends:
                    copy_unit(slot)
                for op, n in AUX.get(s, []):
                    aux(op, n)
                if slot.opens:
                    split(slot.panel + 1)
            def branch_split(q, g):
                slot, n = branch_ring(g + 1)
                act.wait_ge(raw_loaded[slot], branch_loaded(q, g + 1))
                act.wait_ge(unit_done, UNITS1 + 4 * q + 2 * g)
                nc.scalar.activation(whi[:, slot, 0:n], raw[:, slot, 0:n], ACT.Copy).then_inc(hi_ready, 1)

            def merged_hi(q):
                for m in range(2):
                    act.wait_ge(merged, 2 * q + m + 1)
                    nc.scalar.activation(xhi[:, bass.ds(2 * q + m, 1), :], tmp[:, m:m + 1, :], ACT.Copy, scale=0.5)\
                        .then_inc(mhi_ready, 1)

            split(BRANCH0 + 1)
            split(BRANCH0 + 2)
            merged_hi(0)
            with act.Fori(1, KD // 2) as q:
                for g in range(2):
                    branch_split(q, g)
                merged_hi(q)

            def row_squares(job, t, jk, y):
                i = wide_order(job, t)
                tt = job.tiles[t]
                k = rows(tt)
                src = ps[0:k, job.banks[t], :]
                act.wait_ge(wide_done, i)
                if tt == 0:
                    nc.scalar.activation(jk[0:k, 512:1024], ps[DEC:2 * DEC, job.banks[t], :], ACT.Copy).then_inc(sample_low, 1)
                    act.wait_ge(sample_summed, sample_order(job))
                    src = y[0:k, 0, 512 * job.n:512 * job.n + 512]
                nc.scalar.activation(jk[0:k, 0:512], src, ACT.Square,
                                     accum_out=wsq[0:k, 2 * tt + job.n:2 * tt + job.n + 1]).then_inc(wide_squared, 1)
                act.wait_ge(wide_squared, i)

            def row_root(tt, n, base):
                act.wait_ge(first_half, base + tt + 1)
                k = rows(tt)
                nc.scalar.activation(wsum[0:k, tt:tt + 1], wsq[0:k, 2 * tt + n:2 * tt + n + 1], ACT.Sqrt, scale=1.0 / D,
                                     bias=wfirst[0:k, tt:tt + 1]).then_inc(yroot_ready, 1)

            def second_squares(tt):
                act.wait_ge(x1_ready, tt + 1)
                k = rows(tt)
                nc.scalar.activation(junk[0:k, :], x_re[0:k, tt, :], ACT.Square, accum_out=ssq[0:k, tt:tt + 1]).then_inc(x1_sq, 1)
                act.wait_ge(x1_sq, tt + 1)
                nc.scalar.activation(rstd[0:k, tt:tt + 1], ssq[0:k, tt:tt + 1], ACT.Sqrt, scale=1.0 / D, bias=eps[0:k, :])\
                    .then_inc(xroot_ready, 1)

            def second_hi(tt):
                k = rows(tt)
                for kh in range(2):
                    act.wait_ge(x2_turned, 2 * tt + kh + 1)
                    nc.scalar.activation(xhi[:, 4 * kh:4 * kh + 4, tok(tt).start:tok(tt).start + k],
                                         ps[:, TURN_BANKS[tt][kh], :].rearrange("p (k c) -> p k c", k=4)[:, :, 0:k], ACT.Copy)\
                        .then_inc(x2hi_ready, 1)

            preload_sqrt()
            for what, *n in OUT_PLAN:
                if what == "split":
                    split(n[0])
                elif what == "evac":
                    row_squares(OUT_JOBS[n[0]], n[1], junk, y_tok)
                elif what == "residual":
                    row_root(n[0], SECOND_HALF[n[0]], 0)
                elif what == "norm":
                    second_squares(n[0])
                else:
                    second_hi(n[0])

            def up_split(i, r):
                slot = up_slot(r)
                act.wait_ge(raw_loaded[slot], up_loaded(i, r))
                act.wait_ge(unit_done, UNITS2 + 4 * i + 2 * r - 2)
                nc.scalar.activation(whi[:, slot, :], raw[:, slot, :], ACT.Copy).then_inc(hi_ready, 1)

            def up_rows(i, r, first=False, down=None):
                j = 2 * i + r
                for g, h in enumerate((ha, hb)):
                    pair = 4 * (1 - r) + 2 * g
                    act.wait_ge(unit_done, UNITS2 + 2 * j + g + 1)
                    if not first:
                        act.wait_ge(ca_ready, 2 * j + g - 3)
                        act.wait_ge(tails_saved, 4 * j + 2 * g - 6)
                    nc.scalar.activation(h[:, r, 2:2 + DEC], ps[:, pair, 0:DEC], ACT.Copy)
                    nc.scalar.activation(h[:, r, 4 + DEC:4 + HALF], ps[:, pair, DEC:HALF], ACT.Copy)
                    nc.scalar.activation(h[:, r, 4 + HALF:CU], ps[:, pair + 1, 0:HALF], ACT.Copy).then_inc(h_ready, 1)
                if down is None:
                    up_split(i + 1, r)
                else:
                    split(down)
                act.wait_ge(ca_ready, 2 * j + 1)
                nc.scalar.activation(ca[:, 0:UW], ca[:, 0:UW], ACT.Gelu_apprx_tanh).then_inc(gelu_ready, 1)
                act.wait_ge(u_ready, j + 1)
                nc.scalar.activation(uhi[:, bass.ds(j, 1), :], ca[:, 0:UW].rearrange("p (o c) -> p o c", o=1), ACT.Copy).then_inc(uhi_ready, 1)

            act.wait_ge(x1_saved, 16 * TILES)
            for r in range(2):
                up_rows(0, r, first=True)
            with act.Fori(1, KF // 2 - 1) as i:
                for r in range(2):
                    up_rows(i, r)
            for r in range(2):
                up_rows(KF // 2 - 1, r, down=DOWN0 + r)
            preload_sqrt()
            for q, job in enumerate(DOWN_JOBS):
                if q:
                    split(job.panel + 1)
                if q == 1:
                    act.wait_ge(tails_turned, 1)
                    nc.scalar.activation(conv_rows[0:4 * KF, :, :], ps[0:4 * KF, TAILS_BANK, 0:256].rearrange("p (a b) -> p a b", a=2), ACT.Copy)\
                        .then_inc(tails_ready, 1)
                if job.last:
                    for t in range(TILES):
                        row_squares(job, t, junk2, y2_tok)
                        if job.n == 1:
                            row_root(t, 1, TILES)

        @block.vector
        def _(dve):
            chain = [0]

            def link(ins):
                chain[0] += 1
                ins.then_inc(dve_chain, 1)
                dve.wait_ge(dve_chain, chain[0])

            def split(p):
                if p >= NP:
                    return
                dve.wait_ge(hi_ready, p + 1)
                n = panel_size(p)
                nc.vector.tensor_tensor(wlo[:, p % 2, 0:n], raw[:, p % 2, 0:n], whi[:, p % 2, 0:n].bitcast(F32),
                                        ALU.subtract).then_inc(lo_ready, 1)

            def feat(ap):
                return ap.rearrange("p (a b) -> p a b", a=2)

            def head(tt):
                k = rows(tt)
                c = slice(tt, tt + 1)
                dve.wait_ge(root_ready, tt + 1)
                link(nc.vector.reciprocal(rstd[:, c], rstd[:, c]))
                if tt == 0:
                    dve.wait_ge(gpre_loaded, 16)
                nc.vector.scalar_tensor_tensor(out=x_tok[0:k, tt, :], in0=x_tok[0:k, tt, :], scalar=rstd[0:k, c],
                                               in1=gpre[0:k, :], op0=ALU.mult, op1=ALU.mult).then_inc(xn_ready, 1)

            def rest(tt):
                for kh in range(2):
                    t = 2 * tt + kh
                    k = rows(tt)
                    dve.wait_ge(xhi_ready, t + 1)
                    c = slice(tok(tt).start, tok(tt).start + k)
                    nc.vector.tensor_tensor(xlo[:, 4 * kh:4 * kh + 4, c], ps[:, 5 + t % 3, :].rearrange("p (k c) -> p k c", k=4)[:, :, 0:k],
                                            xhi[:, 4 * kh:4 * kh + 4, c].bitcast(F32), ALU.subtract).then_inc(xlo_ready, 1)

            nc.vector.memset(eps, EPS).then_inc(stats_primed, 1)
            nc.vector.memset(ssq, 1.0).then_inc(stats_primed, 1)
            head(0)
            for tt in range(1, TILES):
                head(tt)
                rest(tt - 1)
                if tt == 1:
                    split(0)
            rest(TILES - 1)
            split(1)
            split(2)
            dve.wait_ge(kv_copied, TILES)
            link(nc.vector.tensor_scalar(iws[:, :, :], kvi[:, :, 384:388], IDX_SCALE, None, ALU.mult))

            def gla_update(stream, chunk):
                for h in range(GH):
                    ins = nc.vector.scalar_tensor_tensor(
                        out=state[:, stream, h, :], in0=state[:, stream, h, :], scalar=ebl[:, h, chunk:chunk + 1],
                        in1=ps[:, 4 + h // 2, 256 * (h % 2):256 * (h % 2) + 256], op0=ALU.mult, op1=ALU.add)
                ins.then_inc(state_ready, 1)

            def aux(op, n):
                if op == "coef":
                    dve.wait_ge(coefs_ready, 1)
                    link(nc.vector.tensor_scalar(gnh, col_hn, 0.5, None, ALU.mult))
                elif op == "idx":
                    tt = IDX_TILES[n]
                    w = width(tt)
                    sc = score[n]
                    dve.wait_ge(relu_ready, 4 * n + 1)
                    link(nc.vector.tensor_scalar(sc[:, :], relus[:, 0, 0:w], iws[:, tt, 0:1], None, ALU.mult))
                    for h in range(1, IH):
                        dve.wait_ge(relu_ready, 4 * n + h + 1)
                        ins = nc.vector.scalar_tensor_tensor(out=sc[:, :], in0=relus[:, h, 0:w], scalar=iws[:, tt, h:h + 1],
                                                             in1=sc[:, :], op0=ALU.mult, op1=ALU.add)
                        if h < IH - 1 or tt:
                            link(ins)
                    if tt:
                        ins = nc.vector.memset(sc[0:CHUNK, w - CHUNK:w], BARRED)
                    ins.then_inc(scored, 1)
                    dve.wait_ge(scored, n + 1)
                elif op == "topk":
                    for i, r in n:
                        sc = score[i]
                        link(nc.vector.max(m8, sc[:, :]))
                        link(nc.vector.match_replace(sc[:, :], m8, sc[:, :], TAKEN))
                        if r == (TOPK_S if IDX_TILES[i] == 0 else TOPK_P) // 8 - 1:
                            link(nc.vector.tensor_scalar(sc[:, :], sc[:, :], TAKEN, -BIG, ALU.not_equal, ALU.mult))
                elif op == "att":
                    if n < NATT:
                        tt = ATT_TILES[n // QH]
                        w = width(tt)
                        bias = bias0 if tt == 1 else score[IDX_TILES.index(tt)]
                        dve.wait_ge(logits_done, n + 1)
                        if n == 0:
                            dve.wait_ge(pads_zero, 6)
                        if n >= 3:
                            dve.wait_ge(probs_turned, n - 2)
                        nc.vector.tensor_tensor_reduce(out=lg[:, n % 3, 0:w], in0=ps[:, 4 + n % 2, 0:w], in1=bias[:, 0:w],
                                                       scale=-HD ** -0.5, scalar=3.0e38, op0=ALU.add, op1=ALU.min,
                                                       accum_out=negmax[:, n % 3:n % 3 + 1]).then_inc(masked, 1)
                    m = n - 3
                    if 0 <= m < NATT:
                        h = m % QH
                        dve.wait_ge(probs_ready, m + 1)
                        link(nc.vector.reciprocal(rinv[:, m % 2:m % 2 + 1], rowsum[:, m % 4:m % 4 + 1]))
                        dve.wait_ge(pv_done, m + 1)
                        if m >= QH and h == 0:
                            dve.wait_ge(o_turned, m // QH)
                        g = h // (QH // KVH)
                        nc.vector.tensor_scalar(otok[:, HD * h:HD * h + HD], ps[:, 7, HD * g:HD * g + HD],
                                                rinv[:, m % 2:m % 2 + 1], None, ALU.mult).then_inc(o_scaled, 1)
                elif op == "scan":
                    z, a, b = tmp[:, 0, :], tmp[:, 1, :], tmp[:, 2, :]
                    dve.wait_ge(soft_ready, n + 1)
                    link(nc.vector.scalar_tensor_tensor(out=z, in0=z, scalar=0.0, in1=a, op0=ALU.min, op1=ALU.subtract))
                    link(nc.vector.tensor_tensor_scan(a, restart[:, :], z, 0.0, ALU.mult, ALU.add))
                    ac = a.rearrange("p (n c) -> p n c", c=CHUNK)
                    nc.vector.tensor_tensor(b.rearrange("p (n c) -> p n c", c=CHUNK),
                                            ac[:, :, CHUNK - 1:CHUNK].to_broadcast([P, NCH, CHUNK]), ac, ALU.subtract).then_inc(diff_ready, 1)
                elif op == "apply":
                    z, a, b = tmp[:, 0, :], tmp[:, 1, :], tmp[:, 2, :]
                    dve.wait_ge(decay_exp, 3 * n + 1)
                    nc.vector.tensor_tensor(krem[:, n, :], gk[:, n, :], b, ALU.mult).then_inc(decay_used, 1)
                    dve.wait_ge(decay_exp, 3 * n + 2)
                    nc.vector.tensor_tensor(gq[:, n, :], gq[:, n, :], z, ALU.mult).then_inc(decay_used, 1)
                    dve.wait_ge(decay_exp, 3 * n + 3)
                    nc.vector.tensor_tensor(gk[:, n, :], gk[:, n, :], a, ALU.mult).then_inc(decay_used, 1)
                elif op == "gla":
                    step, tt = GLA_STEPS[n]
                    if step == "a":
                        dve.wait_ge(gla_a, tt + 1)
                        dve.wait_ge(pads_zero, 11)
                        nc.vector.copy_predicated(scm[:, :, :], cmask[:, :, :].bitcast(U32),
                                                  ps[:, 5, :].rearrange("p (h c) -> p h c", h=GH)).then_inc(sc_masked, 1)
                    elif step == "b":
                        dve.wait_ge(gla_b, tt + 1)
                        gla_update(0 if tt == 0 else 1, 0 if tt == 0 else 2 * tt - 1)
                    else:
                        dve.wait_ge(gla_c, tt)
                        dve.wait_ge(state_ready, 2 * tt)
                        gla_update(1, 2 * tt)
                elif op == "scale":
                    rs = tmp[:, 2, :]
                    dve.wait_ge(head_root, n + 1)
                    link(nc.vector.reciprocal(rs, rs))
                    dve.wait_ge(silu_loaded, 16 * (n + 1))
                    for d in range(2):
                        y = got[:, 2 * n + d, :]
                        link(nc.vector.tensor_tensor(y, y, rs, ALU.mult))
                        ins = nc.vector.scalar_tensor_tensor(out=y, in0=y, scalar=gnh[:, d:d + 1], in1=silu_in[:, d, :],
                                                             op0=ALU.mult, op1=ALU.mult)
                    ins.then_inc(head_out, 1)
                elif op == "gsplit":
                    dve.wait_ge(ghi_ready, n + 1)
                    nc.vector.tensor_tensor(glo[:, 2 * n:2 * n + 2, :], got[:, 2 * n:2 * n + 2, :],
                                            ghi[:, 2 * n:2 * n + 2, :].bitcast(F32), ALU.subtract).then_inc(glo_ready, 1)
                elif op == "dsplit":
                    dve.wait_ge(dhi_ready, 1)
                    nc.vector.tensor_tensor(dlo[:, :, :], aqt[:, :, :], dhi[:, :, :].bitcast(F32), ALU.subtract).then_inc(dlo_ready, 1)

            for s, slot in enumerate(SLOTS):
                if slot.kind == "gr" and slot.ends:
                    pair = 2 * (slot.unit % 2)
                    dve.wait_ge(tanh_ready, slot.i + 1)
                    st = feat(stage[:, slot.i % 2, :])
                    nc.vector.scalar_tensor_tensor(out=st, in0=st, scalar=1.0, in1=ps[:, pair:pair + 2, 0:HALF],
                                                   op0=ALU.add, op1=ALU.mult).then_inc(unit_free[slot.unit % 2], 1)
                for op, n in AUX.get(s, []):
                    aux(op, n)
                if slot.opens:
                    split(slot.panel + 1)
            def branch_split(q, g):
                slot, n = branch_ring(g + 1)
                dve.wait_ge(hi_ready, BRANCH0 + 2 * q + g + 2)
                nc.vector.tensor_tensor(wlo[:, slot, 0:n], raw[:, slot, 0:n], whi[:, slot, 0:n].bitcast(F32), ALU.subtract)\
                    .then_inc(lo_ready, 1)

            def merge(q, first=False):
                for g in range(2):
                    branch_split(q, g)
                    for m in range(2):
                        b = (UNITS1 + m) % 2
                        dve.wait_ge(unit_done, UNITS1 + 4 * q + 2 * g + m + 1)
                        if m == 0:
                            dve.wait_ge(gates_loaded[g], 16 * q + 16)
                        if g == 0 and not first:
                            dve.wait_ge(mhi_ready, 2 * q + m - 1)
                            dve.wait_ge(mlo_ready, 2 * q + m - 1)
                        if m == 1 and g == 1:
                            dve.wait_ge(merged, 2 * q + 1)
                        dst = tmp[:, m if g == 0 else 2, :]
                        nc.vector.scalar_tensor_tensor(out=feat(dst), in0=feat(gates_in[:, 2 * g + m, :]), scalar=1.0,
                                                       in1=ps[:, 2 * b:2 * b + 2, 0:HALF], op0=ALU.add, op1=ALU.mult)\
                            .then_inc(unit_free[b], 1)
                        if g == 1:
                            dve.wait_ge(unit_free[b], (UNITS1 + m) // 2 + 2 * q + 2)
                            f = tmp[:, m, :]
                            nc.vector.tensor_tensor(f, f, tmp[:, 2, :], ALU.add).then_inc(merged, 1)
                for m in range(2):
                    dve.wait_ge(mhi_ready, 2 * q + m + 1)
                    for dst, n in ((xsample, DEC), (xlo, T)):
                        block_m = bass.ds(2 * q + m, 1)
                        ins = nc.vector.scalar_tensor_tensor(out=dst[:, block_m, 0:n], in0=tmp[:, m:m + 1, 0:n], scalar=0.5,
                                                             in1=xhi[:, block_m, 0:n].bitcast(F32), op0=ALU.mult, op1=ALU.subtract)
                    ins.then_inc(mlo_ready, 1)

            merge(0, first=True)
            with dve.Fori(1, KD // 2) as q:
                merge(q)

            def wide_copy(job, t, y, gain, low, first):
                tt = job.tiles[t]
                c = slice(512 * job.n, 512 * job.n + 512)
                k = rows(tt)
                src = ps[0:k, job.banks[t], :]
                if tt == 0:
                    dve.wait_ge(sample_low, sample_order(job))
                    nc.vector.tensor_tensor(y[0:k, 0, c], src, low[0:k, 512:1024], ALU.add).then_inc(sample_summed, 1)
                    src = y[0:k, 0, c]
                dve.wait_ge(wide_squared, wide_order(job, t))
                nc.vector.tensor_tensor(y[0:k, tt, c], src, gain[0:k, c], ALU.mult).then_inc(wide_free, 1)
                if first:
                    h = 2 * tt + job.n
                    nc.vector.tensor_scalar(wfirst[0:k, tt:tt + 1], wsq[0:k, h:h + 1], 1.0 / D, EPS, ALU.mult, ALU.add).then_inc(first_half, 1)

            def row_scale(tt, base, copied):
                dve.wait_ge(wide_free, copied)
                dve.wait_ge(yroot_ready, base + tt + 1)
                k = rows(tt)
                link(nc.vector.reciprocal(wsum[0:k, tt:tt + 1], wsum[0:k, tt:tt + 1]))

            def residual(tt, copied):
                k = rows(tt)
                row_scale(tt, 0, copied)
                nc.vector.scalar_tensor_tensor(out=x_re[0:k, tt, :], in0=y_tok[0:k, tt, :], scalar=wsum[0:k, tt:tt + 1],
                                               in1=x_re[0:k, tt, :], op0=ALU.mult, op1=ALU.add).then_inc(x1_ready, 1)

            def second_norm(tt):
                k = rows(tt)
                dve.wait_ge(xroot_ready, tt + 1)
                link(nc.vector.reciprocal(rstd[0:k, tt:tt + 1], rstd[0:k, tt:tt + 1]))
                if tt >= 2:
                    dve.wait_ge(x2_turned, 2 * tt - 2)
                nc.vector.scalar_tensor_tensor(out=xn_tok[0:k, tt % 2, :], in0=x_re[0:k, tt, :], scalar=rstd[0:k, tt:tt + 1],
                                               in1=gffn[0:k, :], op0=ALU.mult, op1=ALU.mult).then_inc(xn2_ready, 1)

            def second_lo(tt):
                k = rows(tt)
                for kh in range(2):
                    c = slice(tok(tt).start, tok(tt).start + k)
                    dve.wait_ge(x2hi_ready, 2 * tt + kh + 1)
                    nc.vector.tensor_tensor(xlo[:, 4 * kh:4 * kh + 4, c],
                                            ps[:, TURN_BANKS[tt][kh], :].rearrange("p (k c) -> p k c", k=4)[:, :, 0:k],
                                            xhi[:, 4 * kh:4 * kh + 4, c].bitcast(F32), ALU.subtract).then_inc(x2lo_ready, 1)

            dve.wait_ge(posts_loaded, 32)
            closed = 0
            for what, *n in OUT_PLAN:
                if what == "split":
                    split(n[0])
                elif what == "evac":
                    wide_copy(OUT_JOBS[n[0]], n[1], y_tok, gpost, junk, OUT_JOBS[n[0]].n != SECOND_HALF[OUT_JOBS[n[0]].tiles[n[1]]])
                    closed += 1
                elif what == "residual":
                    if n[0] == 0:
                        dve.wait_ge(x_reloaded, 16 * TILES)
                    residual(n[0], closed)
                elif what == "norm":
                    second_norm(n[0])
                else:
                    second_lo(n[0])

            def up_split(i, r):
                slot = up_slot(r)
                dve.wait_ge(hi_ready, UP0 + 2 * i + r + 1)
                nc.vector.tensor_tensor(wlo[:, slot, :], raw[:, slot, :], whi[:, slot, :].bitcast(F32), ALU.subtract).then_inc(lo_ready, 1)

            def up_conv(i, r, first=False, down=None):
                j = 2 * i + r
                for g, (h, c) in enumerate(((ha, ca), (hb, cb))):
                    b = bass.ds(j + KF * g, 1)
                    dve.wait_ge(h_ready, 2 * j + g + 1)
                    dve.wait_ge(rim_ready, 2 * j + g + 1)
                    if g == 0 and not first:
                        dve.wait_ge(uhi_ready, j)
                        dve.wait_ge(ulo_ready, j)
                    cc = c[:, 0:UW]
                    hr = h[:, r, :]
                    nc.vector.tensor_scalar(cc, hr[:, 2:CU], cw2[:, b], cbias[:, b], ALU.mult, ALU.add).then_inc(taps_done, 1)
                    dve.wait_ge(taps_done, 4 * j + 2 * g + 1)
                    nc.vector.scalar_tensor_tensor(out=cc, in0=hr[:, 1:CU - 1], scalar=cw1[:, b], in1=cc, op0=ALU.mult, op1=ALU.add)\
                        .then_inc(taps_done, 1)
                    dve.wait_ge(taps_done, 4 * j + 2 * g + 2)
                    nc.vector.scalar_tensor_tensor(out=cc, in0=hr[:, 0:CU - 2], scalar=cw0[:, b], in1=cc, op0=ALU.mult, op1=ALU.add)\
                        .then_inc(ca_ready, 1)
                if down is None:
                    up_split(i + 1, r)
                else:
                    split(down)
                dve.wait_ge(gelu_ready, j + 1)
                dve.wait_ge(ca_ready, 2 * j + 2)
                nc.vector.tensor_tensor(ca[:, 0:UW], ca[:, 0:UW], cb[:, :], ALU.mult).then_inc(u_ready, 1)
                dve.wait_ge(uhi_ready, j + 1)
                for dst, c0, n in ((usample, 0, DEC), (ulo, DEC + 2, SEQ)):
                    ins = nc.vector.tensor_tensor(dst[:, bass.ds(j, 1), 0:n], ca[:, c0:c0 + n].rearrange("p (o c) -> p o c", o=1),
                                                  uhi[:, bass.ds(j, 1), c0:c0 + n].bitcast(F32), ALU.subtract)
                ins.then_inc(ulo_ready, 1)

            dve.wait_ge(pads_zero, 15)
            for r in range(2):
                up_conv(0, r, first=r == 0)
            with dve.Fori(1, KF // 2 - 1) as i:
                for r in range(2):
                    up_conv(i, r)
            for r in range(2):
                up_conv(KF // 2 - 1, r, down=DOWN0 + r)
            for q, job in enumerate(DOWN_JOBS):
                if q:
                    split(job.panel + 1)
                if job.last:
                    for t in range(TILES):
                        if job.n == 0 and t == 0:
                            dve.wait_ge(gfin_loaded, 16)
                        wide_copy(job, t, y2_tok, gfin, junk2, job.n == 0)
                        if job.n == 1:
                            k = rows(t)
                            row_scale(t, TILES, wide_order(job, t))
                            dve.wait_ge(x1_loaded[t % 4], 16 * (t // 4 + 1))
                            nc.vector.scalar_tensor_tensor(out=y2_tok[0:k, t, :], in0=y2_tok[0:k, t, :], scalar=wsum[0:k, t:t + 1],
                                                           in1=x1_back[t % 4][0:k, :], op0=ALU.mult, op1=ALU.add).then_inc(out_ready, 1)

        @block.tensor
        def _(pe):
            def open_panel(p):
                pe.wait_ge(lo_ready, p + 1)

            def half_of(w, p, k, n):
                return w[:, p % 2, 0:k * n].rearrange("p (k n) -> p k n", k=k)

            def stationary_weights(out, p, kn, n, c0, xh, xl, t):
                wh, wl = half_of(whi, p, kn, n), half_of(wlo, p, kn, n)
                for k in range(kn):
                    pe.matmul(out, wh[:, k, c0:c0 + P], xh[:, k, t], start=(k == 0), stop=False)
                    pe.matmul(out, wh[:, k, c0:c0 + P], xl[:, k, t], start=False, stop=False)
                    ins = pe.matmul(out, wl[:, k, c0:c0 + P], xh[:, k, t], start=False, stop=(k == kn - 1))
                return ins

            def moving_weights(out, p, k0, kn, n, xh, xl, t, first, last, tl=None):
                wh, wl = half_of(whi, p, kn, n), half_of(wlo, p, kn, n)
                for k in range(kn):
                    pe.matmul(out, xh[:, k0 + k, t], wh[:, k, :], start=(first and k == 0), stop=False)
                    pe.matmul(out, xl[:, k0 + k, tl or t], wh[:, k, :], start=False, stop=False)
                    ins = pe.matmul(out, xh[:, k0 + k, t], wl[:, k, :], start=False, stop=(last and k == kn - 1))
                return ins

            def moving_sample(out, p, k0, kn, n, both, first, last):
                wh, wl = half_of(whi, p, kn, n), half_of(wlo, p, kn, n)
                for k in range(kn):
                    pe.matmul(out, both[:, k0 + k, :], wh[:, k, :], start=(first and k == 0), stop=False)
                    ins = pe.matmul(out, both[:, k0 + k, :], wl[:, k, :], start=False, stop=(last and k == kn - 1))
                return ins

            def turn(tt):
                k = rows(tt)
                pe.wait_ge(xn_ready, tt + 1)
                for kh in range(2):
                    t = 2 * tt + kh
                    if t >= 3:
                        pe.wait_ge(xlo_ready, t - 2)
                    for j in range(4):
                        f = 4 * kh + j
                        ins = pe.transpose(ps[:, 5 + t % 3, P * j:P * j + k], x_tok[0:k, tt, P * f:P * f + P], ident[0:k, 0:k])
                    ins.then_inc(x_turned, 1)

            def keys_values(p, tt):
                if tt == 0:
                    open_panel(p)
                pe.wait_ge(xlo_ready, 2 * max(tt, 1) + 2)
                return moving_weights(ps[:, tt, 0:340], p, 4 * p, 4, 340, xhi, xlo, tok(tt), p == 0, p == 1)

            pe.wait_ge(consts_ready, 1)
            turn(0)
            turn(1)
            for tt in range(TILES):
                if tt + 2 < TILES:
                    turn(tt + 2)
                ins = keys_values(0, tt)
            ins.then_inc(panel_used, 1)
            for tt in range(TILES):
                keys_values(1, tt).then_inc(kv_done, 1)

            def main(slot):
                u = slot.unit
                pair = 2 * (u % 2)
                if slot.opens:
                    open_panel(slot.panel)
                starts = slot.part % 2 == 0
                if starts:
                    unit_waits(pe, u)
                    if u < 2:
                        pe.wait_ge(kv_copied, 2 * u + 2)
                if slot.kind == "z":
                    for j in range(2):
                        ins = pe.matmul(ps[:, pair + j, 0:HALF], wgu[:, P * slot.i:P * slot.i + P],
                                        glow[:, HALF * j:HALF * j + HALF], start=True, stop=True)
                elif slot.kind == "gv":
                    ins = moving_weights(ps[:, pair + slot.part % 2, 0:256], slot.panel, 0, KD, 256, xhi, xlo,
                                         tok(slot.part), True, True)
                else:
                    ins = stationary_weights(ps[:, pair + slot.part, 0:HALF], slot.panel, KD, 256, P * (slot.i % 2),
                                             xhi, xlo, slice(HALF * slot.part, HALF * slot.part + HALF))
                if slot.ends:
                    ins.then_inc(unit_done, 1)

            def state_products(kr, tt):
                for h in range(GH):
                    ins = pe.matmul(ps[:, 4 + h // 2, 256 * (h % 2):256 * (h % 2) + 256], kr[:, h, :],
                                    v_tok[:, tt, 256 * h:256 * h + 256], start=True, stop=True)
                return ins

            def outputs_of_state(stream, q, last):
                for h in range(GH):
                    for d in range(2):
                        r = 2 * (h % 2) + d
                        ins = pe.matmul(ps[:, 6 + h // 2, P * r:P * r + P], state[:, stream, h, P * d:P * d + P], q[:, h, :],
                                        start=False, stop=last, skip_group_check=True)
                return ins

            def aux(op, n):
                if op == "coef":
                    pe.wait_ge(coefs_loaded, 16 * 8)
                    pe.transpose(ps[:, 7, 0:94], coef_rows[0:94, 0, :], ident[0:94, 0:94])
                    pe.transpose(ps[:, 7, 96:184], coef_rows[0:88, 1, :], ident[0:88, 0:88])
                    pe.transpose(ps[:, 7, 184:272], coef_rows[0:88, 2, :], ident[0:88, 0:88]).then_inc(coefs_turned, 1)
                elif op == "keyt":
                    pe.wait_ge(coefs_ready, 1)
                    pe.wait_ge(consts_ready, 4)
                    pe.wait_ge(kv_copied, TILES)
                    pe.wait_ge(cache_loaded, 16 * 4)
                    for tt in range(1, TILES):
                        c = slice(P * (tt - 1), P * tt)
                        pe.transpose(ps[:, 5, c], kvi[:, tt, 0:128], ident[:, :])
                        pe.transpose(ps[:, 6, c], kvi[:, tt, 256:384], ident[:, :])
                        pe.transpose(ps[0:RANK, 4, c], kvi[:, tt, 388:404], ident[:, :])
                    i64 = ident[0:DEC, 0:DEC]
                    pe.transpose(ps[:, 7, 0:128], cache[:, 0, :], ident[:, :])
                    pe.transpose(ps[:, 7, 128:192], kvi[0:DEC, 0, 0:128], i64)
                    pe.transpose(ps[:, 7, 192:320], cache[:, 2, :], ident[:, :])
                    pe.transpose(ps[:, 7, 320:384], kvi[0:DEC, 0, 256:384], i64)
                    pe.transpose(ps[0:RANK, 7, 384:448], kvi[0:DEC, 0, 388:404], i64).then_inc(keys_turned, 1)
                elif op == "idx":
                    tt = IDX_TILES[n]
                    w = width(tt)
                    if n == 0:
                        pe.wait_ge(keys_ready, 1)
                        pe.wait_ge(unit_free[0], 1)
                        pe.wait_ge(unit_free[1], 1)
                    else:
                        pe.wait_ge(relu_ready, 4 * n)
                    for h in range(IH):
                        ins = pe.matmul(ps[:, 4 + h, 0:w], iqt[:, h // 2, tok(tt)], iz[:, h % 2, keys(tt)], start=True, stop=True)
                    ins.then_inc(dots_done, 1)
                elif op == "att":
                    if n < NATT:
                        tt = ATT_TILES[n // QH]
                        w = width(tt)
                        h = n % QH
                        if n == 0:
                            pe.wait_ge(unit_free[0], 3)
                            pe.wait_ge(unit_free[1], 3)
                            pe.wait_ge(relu_ready, 4 * len(IDX_TILES))
                            pe.wait_ge(scored, len(IDX_TILES))
                        if n >= 2:
                            pe.wait_ge(masked, n - 1)
                        if n >= 12 and (n - 5) % QH == QH - 1:
                            pe.wait_ge(o_ready, (n - 5) // QH + 1)
                        pe.matmul(ps[:, 4 + n % 2, 0:w], aqt[:, h % 4, tok(tt)], kz[:, h // 4, keys(tt)],
                                  start=True, stop=True).then_inc(logits_done, 1)
                    m = n - 2
                    if 0 <= m < NATT:
                        pe.wait_ge(probs_ready, m + 1)
                        if m >= 1:
                            pe.wait_ge(pt_ready, m)
                        for i, (c, k) in enumerate(key_blocks(ATT_TILES[m // QH])):
                            ins = pe.transpose(ps[0:k, 6, P * i:P * i + P], lg[:, m % 3, c:c + k], ident[:, :])
                        ins.then_inc(probs_turned, 1)
                    m = n - 3
                    if 0 <= m < NATT:
                        tt = ATT_TILES[m // QH]
                        pe.wait_ge(pt_ready, m + 1)
                        if m >= 1:
                            pe.wait_ge(o_scaled, m)
                        blocks = key_blocks(tt)
                        for i, (c, k) in enumerate(blocks):
                            if tt == 0:
                                val = cache[:, 1, :] if i == 0 else kvi[0:DEC, 0, 128:256]
                            else:
                                val = kvi[:, i + 1, 128:256]
                            ins = pe.matmul(ps[:, 7, 0:128], pt[0:k, m % 2, P * i:P * i + P], val,
                                            start=(i == 0), stop=(i == len(blocks) - 1))
                        ins.then_inc(pv_done, 1)
                    m = n - 4
                    if m >= 0 and m % QH == QH - 1:
                        pe.wait_ge(o_scaled, m + 1)
                        for b in range(4):
                            ins = pe.transpose(ps[:, 4 + (n + 1) % 2, P * b:P * b + P], otok[:, P * b:P * b + P], ident[:, :])
                        ins.then_inc(o_turned, 1)
                elif op == "gla":
                    step, tt = GLA_STEPS[n]
                    stream = 0 if tt == 0 else 1
                    if step == "a":
                        if n == 0:
                            pe.wait_ge(decay_used, 3 * GH)
                            pe.wait_ge(o_ready, len(ATT_TILES))
                        else:
                            pe.wait_ge(state_ready, 1 if tt == 1 else 2 * tt - 1)
                        for h in range(GH):
                            pe.transpose(ps[:, 4, P * h:P * h + P], krem[:, h, tok(tt)], ident[:, :])
                        for h in range(GH):
                            ins = pe.matmul(ps[:, 5, P * h:P * h + P], gk[:, h, tok(tt)], gq[:, h, tok(tt)], start=True, stop=True)
                        ins.then_inc(gla_a, 1)
                    elif step == "b":
                        if tt == 0:
                            pe.wait_ge(state_loaded, 32)
                        if tt >= 1:
                            pe.wait_ge(got_copied, tt)
                            pe.wait_ge(state_ready, 1 if tt == 1 else 2 * tt - 1)
                        pe.wait_ge(sc_masked, tt + 1)
                        pe.wait_ge(q_padded, 2 * tt + 2)
                        for h in range(GH):
                            for d in range(2):
                                r = 2 * (h % 2) + d
                                pe.matmul(ps[:, 6 + h // 2, P * r:P * r + P], v_tok[:, tt, 256 * h + P * d:256 * h + P * d + P],
                                          scm[:, h, :], start=(r == 0), stop=False, skip_group_check=True)
                        outputs_of_state(stream, qa, tt == 0)
                        pe.wait_ge(krem_ready, 2 * tt + 2)
                        state_products(krem_a, tt).then_inc(gla_b, 1)
                    else:
                        pe.wait_ge(state_ready, 2 * tt)
                        outputs_of_state(stream, qb, True)
                        state_products(krem_b, tt).then_inc(gla_c, 1)
                elif op == "norm":
                    pe.wait_ge(sq_ready, n + 1)
                    if n == 0:
                        pe.wait_ge(state_ready, 2 * TILES - 1)
                    else:
                        pe.wait_ge(head_root, n)
                    for j in range(2):
                        for d in range(2):
                            ins = pe.matmul(ps[:, 4 + j, 0:HALF], ones[:, :], tmp[:, d, HALF * j:HALF * j + HALF],
                                            start=(d == 0), stop=(d == 1))
                    ins.then_inc(norm_summed, 1)

            for s, slot in enumerate(SLOTS):
                main(slot)
                for op, n in AUX.get(s, []):
                    aux(op, n)
            pe.wait_ge(glo_ready, GH)
            pe.wait_ge(dlo_ready, 1)
            with pe.Fori(0, KD // 2) as q:
                for g in range(2):
                    pe.wait_ge(lo_ready, BRANCH0 + 1 + g + 2 * q)
                    xh, xl, kn = (ghi, glo, KD) if g == 0 else (dhi, dlo, 4)
                    for m in range(2):
                        u = UNITS1 + 2 * g + m
                        pe.wait_ge(unit_free[u % 2], u // 2 + 2 * q)
                        for j in range(2):
                            ins = stationary_weights(ps[:, 2 * (u % 2) + j, 0:HALF], BRANCH0 + g, kn, 256, P * m, xh, xl,
                                                     slice(HALF * j, HALF * j + HALF))
                        ins.then_inc(unit_done, 1)

            def wide(job, both, xh, xl, prompt_hi, prompt_lo):
                open_panel(job.panel)
                for t, tt in enumerate(job.tiles):
                    if job.first:
                        wait_bank(job, t)
                        if job.panel == DOWN0 and job.banks[t] < 4:
                            pe.wait_ge(h_ready, 2 * KF)
                    if tt == 0:
                        ins = moving_sample(ps[:, job.banks[t], :], job.panel, job.k0, job.kn, 512, both, job.first, job.last)
                    else:
                        ins = moving_weights(ps[:, job.banks[t], :], job.panel, job.k0, job.kn, 512, xh, xl, prompt(tt, prompt_hi),
                                             job.first, job.last, prompt(tt, prompt_lo))
                    if job.last:
                        ins.then_inc(wide_done, 1)
                if not job.last:
                    ins.then_inc(panel_used, 1)

            def wait_bank(job, t):
                before = [wide_order(j, i) for j in JOBS[:JOBS.index(job)] if j.last
                          for i, b in enumerate(j.banks) if b == job.banks[t]]
                if before:
                    pe.wait_ge(wide_free, before[-1])

            def turn_again(tt):
                k = rows(tt)
                pe.wait_ge(xn2_ready, tt + 1)
                pe.wait_ge(wide_free, 10 if tt == 3 else 8 if tt == 4 else 6)
                if tt >= 2:
                    pe.wait_ge(x2lo_ready, {2: 2, 3: 6, 4: 4}[tt])
                for kh in range(2):
                    for j in range(4):
                        f = 4 * kh + j
                        ins = pe.transpose(ps[:, TURN_BANKS[tt][kh], P * j:P * j + k], xn_tok[0:k, tt % 2, P * f:P * f + P],
                                           ident[0:k, 0:k])
                    ins.then_inc(x2_turned, 1)

            for q, job in enumerate(OUT_JOBS):
                if q == 2:
                    pe.wait_ge(unit_free[0], UNITS2 // 2)
                    pe.wait_ge(unit_free[1], UNITS2 // 2)
                pe.wait_ge(mlo_ready, 8 if job.k0 else 4)
                wide(job, xsample, xhi, xlo, DEC, DEC)
                for tt in {5: (0,), 6: (1, 2)}.get(q, ()):
                    turn_again(tt)

            def up(r, g, t):
                return stationary_weights(ps[:, 4 * (1 - r) + 2 * g + t, 0:HALF], UP0 + r, KD, 256, P * g, xhi, xlo,
                                          slice(HALF * t, HALF * t + HALF))

            pe.wait_ge(x2lo_ready, 6)
            pe.wait_ge(wide_free, 9)
            for j in range(2):
                open_panel(UP0 + j)
                for g in range(2):
                    up(j, g, 0)
                    if (j, g) == (1, 0):
                        turn_again(3)
                        turn_again(4)
            pe.wait_ge(x2lo_ready, 2 * TILES)
            for j in range(2):
                for g in range(2):
                    up(j, g, 1).then_inc(unit_done, 1)
            with pe.Fori(1, KF // 2) as i:
                for r in range(2):
                    pe.wait_ge(lo_ready, UP0 + 2 * i + r + 1)
                    for g in range(2):
                        pe.wait_ge(h_ready, 4 * i + 2 * r + g - 3)
                        up(r, g, 0)
                        up(r, g, 1).then_inc(unit_done, 1)
            pe.wait_ge(h_ready, 2 * KF - 2)
            for q, job in enumerate(DOWN_JOBS):
                pe.wait_ge(ulo_ready, job.k0 + job.kn)
                wide(job, usample, uhi, ulo, DEC + 2, 0)
                if q == 0:
                    pe.wait_ge(tails_saved, 4 * KF)
                    for i in range(2):
                        ins = pe.transpose(ps[0:4 * KF, TAILS_BANK, P * i:P * i + P], convs[:, 2 * i:2 * i + 2, :].rearrange("p a b -> p (a b)"),
                                           ident[:, :])
                    ins.then_inc(tails_turned, 1)
                if q == NG - 1:
                    pe.wait_ge(tails_ready, 1)


_INS = ['x_prompt', 'x_sample', 'cache_k', 'cache_v', 'cache_k_idx', 'state_gla', 'state_ffn_conv', 'attn_pre_norm', 'w_in',
        'w_gla_gate_up', 'b_gla_gate', 'gla_head_norm', 'w_branch_gla', 'w_branch_dsa', 'w_out', 'attn_post_norm',
        'ffn_pre_norm', 'w_up', 'conv_w', 'conv_b', 'w_down', 'ffn_post_norm']
_OUTS = [("y_p", (1, SEQ, D)), ("y_s", (1, DEC, D)),
         ("k_p", (1, 1, SEQ, KVH, HD)), ("v_p", (1, 1, SEQ, KVH, HD)), ("kidx_p", (1, 1, SEQ, ID)),
         ("gla_p", (1, 1, GH, DK, DV)), ("conv_p", (1, 1, CW - 1, 2 * FFN)),
         ("k_s", (1, 1, DEC, KVH, HD)), ("v_s", (1, 1, DEC, KVH, HD)), ("kidx_s", (1, 1, DEC, ID)),
         ("gla_s", (1, 1, GH, DK, DV)), ("conv_s", (1, 1, CW - 1, 2 * FFN))]


def kernel(**inputs):
    import numpy as np
    import concourse.bacc as bacc
    from concourse.bass_utils import run_bass_kernel_spmd

    nc = bacc.Bacc("TRN2", target_bir_lowering=False, num_devices=1)
    arrays, A, O = {}, {}, {}
    for name in _INS:
        a = np.ascontiguousarray(inputs[name])
        arrays[f"in_{name}"] = a
        A[name] = nc.dram_tensor(f"in_{name}", a.shape, F32, kind="ExternalInput").ap()
    for name, shape in _OUTS:
        O[name] = nc.dram_tensor(f"out_{name}", shape, F32, kind="ExternalOutput").ap()
    layer_kernel(nc, A, O)
    r = run_bass_kernel_spmd(nc, [arrays], core_ids=[0])
    return tuple(r.results[0][f"out_{name}"] for name, _ in _OUTS)
```
